# Optimizing a Trainium2 kernel written in Bass

```python
import math
import jax, jax.numpy as jnp
from jax import lax
import numpy as np

D_MODEL = 1024
BATCH = 1
SEQ = 256
DEPTH = 1

D_RNN = 1024
RNN_BLOCKS = 16
RNN_BW = D_RNN // RNN_BLOCKS
CONV_W = 4
LRU_C = 8.0
N_HEADS = 16
N_KV = 4
HEAD_DIM = 64
GROUP = N_HEADS // N_KV
WINDOW = 128
BLOCK_Q = 128
Q_DIM = N_HEADS * HEAD_DIM
KV_DIM = N_KV * HEAD_DIM
N_EXPERTS = 32
TOP_K = 4
D_FF = 1024
SWIGLU_LIMIT = 7.0
SWIGLU_ALPHA = 1.702
MOE_BLOCK = 128
EPS = 1e-6
SPLITS = (D_RNN, D_RNN, Q_DIM, KV_DIM, KV_DIM, D_MODEL, D_MODEL)
D_IN = sum(SPLITS)


def rmsnorm(x, g):
    xf = x.astype(jnp.float32)
    y = xf * lax.rsqrt(jnp.mean(xf * xf, axis=-1, keepdims=True) + EPS)
    return (y * g.astype(jnp.float32)).astype(x.dtype)

def causal_depthwise_conv(x, w, b):
    S = x.shape[1]
    xp = jnp.pad(x, ((0, 0), (CONV_W - 1, 0), (0, 0)))
    y = b
    for kk in range(CONV_W):
        y = y + xp[:, kk:kk + S] * w[kk]
    return y

def rg_lru(x, w_a, b_a, w_x, b_x, lam):
    B, S, _ = x.shape
    xb = x.reshape(B, S, RNN_BLOCKS, RNN_BW)
    gate_r = jax.nn.sigmoid(jnp.einsum('bshi,hij->bshj', xb, w_a).reshape(B, S, D_RNN) + b_a)
    gate_i = jax.nn.sigmoid(jnp.einsum('bshi,hij->bshj', xb, w_x).reshape(B, S, D_RNN) + b_x)
    log_a = -LRU_C * gate_r.astype(jnp.float32) * jax.nn.softplus(-lam.astype(jnp.float32))
    a = jnp.exp(log_a)
    mult = jnp.sqrt(-jnp.expm1(2.0 * log_a))
    reset = (jnp.arange(S) == 0)[None, :, None]
    mult = jnp.where(reset, 1.0, mult)
    bterm = (x * gate_i).astype(jnp.float32) * mult

    def combine(left, right):
        a1, b1 = left
        a2, b2 = right
        return a1 * a2, a2 * b1 + b2

    _, h = lax.associative_scan(combine, (a, bterm), axis=1)
    return h.astype(x.dtype)

def alibi_slopes():
    return np.array([2.0 ** (-8.0 * (h + 1) / N_HEADS) for h in range(N_HEADS)], dtype=np.float32)

def swa_sink_attention(q, k, v, sinks):
    B, S = q.shape[0], q.shape[1]
    nb = S // BLOCK_Q
    qb = q.reshape(B, nb, BLOCK_Q, N_KV, GROUP, HEAD_DIM)
    pad = ((0, 0), (BLOCK_Q, 0), (0, 0), (0, 0))
    kb = jnp.pad(k, pad).reshape(B, nb + 1, BLOCK_Q, N_KV, HEAD_DIM)
    vb = jnp.pad(v, pad).reshape(B, nb + 1, BLOCK_Q, N_KV, HEAD_DIM)
    k_band = jnp.concatenate([kb[:, :-1], kb[:, 1:]], axis=2)
    v_band = jnp.concatenate([vb[:, :-1], vb[:, 1:]], axis=2)
    s = jnp.einsum('bnqkgd,bnckd->bnkgqc', qb, k_band,
                   preferred_element_type=jnp.float32) * (HEAD_DIM ** -0.5)
    qi = jnp.arange(BLOCK_Q)[:, None]
    ci = jnp.arange(2 * BLOCK_Q)[None, :]
    dist = qi + BLOCK_Q - ci
    kpos = jnp.arange(nb)[:, None, None] * BLOCK_Q - BLOCK_Q + ci[None]
    valid = (dist >= 0) & (dist < WINDOW) & (kpos >= 0)
    slopes = jnp.asarray(alibi_slopes()).reshape(N_KV, GROUP)[:, :, None, None]
    s = s - slopes * dist.astype(jnp.float32)
    s = jnp.where(valid[None, :, None, None], s, -jnp.inf)
    sink = sinks.astype(jnp.float32).reshape(N_KV, GROUP)[:, :, None, None]
    m = jnp.maximum(jnp.max(s, axis=-1, keepdims=True), sink)
    p = jnp.exp(s - m)
    denom = jnp.sum(p, axis=-1, keepdims=True) + jnp.exp(sink - m)
    o = jnp.einsum('bnkgqc,bnckd->bnqkgd', (p / denom).astype(v.dtype), v_band)
    return o.reshape(B, S, Q_DIM)

def clamped_swiglu(hid):
    x_glu = jnp.minimum(hid[..., ::2], SWIGLU_LIMIT)
    x_lin = jnp.clip(hid[..., 1::2], -SWIGLU_LIMIT, SWIGLU_LIMIT)
    return x_glu * jax.nn.sigmoid(SWIGLU_ALPHA * x_glu) * (x_lin + 1.0)

def moe_ffn(h, router_w, router_b, w1, b1, w2, b2):
    B, S, D = h.shape
    N = B * S
    xt = h.reshape(N, D)
    logits = (xt @ router_w + router_b).astype(jnp.float32)
    top_v, top_e = lax.top_k(logits, TOP_K)
    gates = jax.nn.softmax(top_v, axis=-1)
    A = N * TOP_K
    e_flat = top_e.reshape(A)
    g_flat = gates.reshape(A)
    tok = jnp.arange(A, dtype=jnp.int32) // TOP_K
    order = jnp.argsort(e_flat, stable=True)
    e_s, tok_s, g_s = e_flat[order], tok[order], g_flat[order]
    counts = jnp.bincount(e_flat, length=N_EXPERTS)
    starts = jnp.cumsum(counts) - counts
    padded = ((counts + MOE_BLOCK - 1) // MOE_BLOCK) * MOE_BLOCK
    pend = jnp.cumsum(padded)
    pstart = pend - padded
    dest = pstart[e_s] + jnp.arange(A, dtype=jnp.int32) - starts[e_s]
    P = A + N_EXPERTS * MOE_BLOCK
    nblk = P // MOE_BLOCK
    tok_buf = jnp.full((P,), N, dtype=jnp.int32).at[dest].set(tok_s)
    g_buf = jnp.zeros((P,), jnp.float32).at[dest].set(g_s)
    blk_e = jnp.clip(jnp.searchsorted(pend, jnp.arange(nblk, dtype=jnp.int32) * MOE_BLOCK,
                                      side='right'), 0, N_EXPERTS - 1)
    x_pad = jnp.concatenate([xt, jnp.zeros((1, D), xt.dtype)], axis=0)
    xb = x_pad[tok_buf].reshape(nblk, MOE_BLOCK, D)

    def expert_block(args):
        xblk, e = args
        act = clamped_swiglu(xblk @ w1[e] + b1[e])
        return act @ w2[e] + b2[e]

    yb = lax.map(expert_block, (xb, blk_e)).reshape(P, D)
    yb = yb * g_buf[:, None].astype(yb.dtype)
    out = jax.ops.segment_sum(yb, tok_buf, num_segments=N + 1)[:N]
    return out.reshape(B, S, D)

def first_inputs(seed: int = 0) -> dict:
    key = jax.random.key(seed)
    ks = jax.random.split(key, 24)
    f32 = jnp.float32
    L = DEPTH

    def nrm(k, shape, scale):
        return jax.random.normal(k, shape, f32) * scale

    def gain(k, shape):
        return 1.0 + 0.05 * jax.random.normal(k, shape, f32)

    u = jax.random.uniform(ks[12], (L, D_RNN), f32, 0.9, 0.999)
    sig = u ** (1.0 / LRU_C)
    rg_lambda = jnp.log(sig) - jnp.log1p(-sig)
    return {
        "x": nrm(ks[0], (BATCH, SEQ, D_MODEL), 1.0),
        "c": nrm(ks[1], (BATCH, D_MODEL), 1.0),
        "w_ada": nrm(ks[2], (L, D_MODEL, 6 * D_MODEL), 0.5 * D_MODEL ** -0.5),
        "b_ada": nrm(ks[3], (L, 6 * D_MODEL), 0.02),
        "norm_pre_mix": gain(ks[4], (L, D_MODEL)),
        "norm_post_mix": gain(ks[5], (L, D_MODEL)),
        "norm_pre_ffn": gain(ks[6], (L, D_MODEL)),
        "norm_post_ffn": gain(ks[7], (L, D_MODEL)),
        "w_in": nrm(ks[8], (L, D_MODEL, D_IN), D_MODEL ** -0.5),
        "b_in": nrm(ks[9], (L, D_IN), 0.02),
        "conv_w": nrm(ks[10], (L, CONV_W, D_RNN), CONV_W ** -0.5),
        "conv_b": nrm(ks[11], (L, D_RNN), 0.02),
        "rg_w_a": nrm(ks[13], (L, RNN_BLOCKS, RNN_BW, RNN_BW), RNN_BW ** -0.5),
        "rg_b_a": nrm(ks[14], (L, D_RNN), 0.02),
        "rg_w_x": nrm(ks[15], (L, RNN_BLOCKS, RNN_BW, RNN_BW), RNN_BW ** -0.5),
        "rg_b_x": nrm(ks[16], (L, D_RNN), 0.02),
        "rg_lambda": rg_lambda,
        "attn_sinks": nrm(ks[17], (L, N_HEADS), 0.5),
        "w_o_rnn": nrm(ks[18], (L, D_RNN, D_MODEL), D_RNN ** -0.5),
        "w_o_attn": nrm(ks[19], (L, Q_DIM, D_MODEL), Q_DIM ** -0.5),
        "w_out": nrm(ks[20], (L, D_MODEL, D_MODEL), D_MODEL ** -0.5),
        "router_w": nrm(ks[21], (L, D_MODEL, N_EXPERTS), D_MODEL ** -0.5),
        "router_b": nrm(ks[22], (L, N_EXPERTS), 0.01),
        "moe_w1": nrm(jax.random.fold_in(ks[23], 0), (L, N_EXPERTS, D_MODEL, 2 * D_FF), D_MODEL ** -0.5),
        "moe_b1": nrm(jax.random.fold_in(ks[23], 1), (L, N_EXPERTS, 2 * D_FF), 0.02),
        "moe_w2": nrm(jax.random.fold_in(ks[23], 2), (L, N_EXPERTS, D_FF, D_MODEL), D_FF ** -0.5),
        "moe_b2": nrm(jax.random.fold_in(ks[23], 3), (L, N_EXPERTS, D_MODEL), 0.02),
    }

def first_block(x, c, w_ada, b_ada, norm_pre_mix, norm_post_mix, norm_pre_ffn, norm_post_ffn,
              w_in, b_in, conv_w, conv_b, rg_w_a, rg_b_a, rg_w_x, rg_b_x, rg_lambda,
              attn_sinks, w_o_rnn, w_o_attn, w_out, router_w, router_b,
              moe_w1, moe_b1, moe_w2, moe_b2):
    B, S, _ = x.shape
    split_points = np.cumsum(np.array(SPLITS))[:-1].tolist()
    for layer in range(DEPTH):
        ada = (jax.nn.silu(c) @ w_ada[layer] + b_ada[layer])[:, None, :]
        sh1, sc1, g1, sh2, sc2, g2 = jnp.split(ada, 6, axis=-1)

        h = rmsnorm(x, norm_pre_mix[layer]) * (1.0 + sc1) + sh1
        proj = h @ w_in[layer] + b_in[layer]
        xr, gr, q, k, v, gate_r, gate_a = jnp.split(proj, split_points, axis=-1)
        xr = causal_depthwise_conv(xr, conv_w[layer], conv_b[layer])
        y_rnn = rg_lru(xr, rg_w_a[layer], rg_b_a[layer], rg_w_x[layer], rg_b_x[layer],
                       rg_lambda[layer]) * jax.nn.gelu(gr)
        y_att = swa_sink_attention(q.reshape(B, S, N_HEADS, HEAD_DIM),
                                   k.reshape(B, S, N_KV, HEAD_DIM),
                                   v.reshape(B, S, N_KV, HEAD_DIM), attn_sinks[layer])
        merged = (jax.nn.sigmoid(gate_r) * (y_rnn @ w_o_rnn[layer])
                  + jax.nn.sigmoid(gate_a) * (y_att @ w_o_attn[layer]))
        mix = merged @ w_out[layer]
        x = x + g1 * rmsnorm(mix, norm_post_mix[layer])

        h = rmsnorm(x, norm_pre_ffn[layer]) * (1.0 + sc2) + sh2
        ff = moe_ffn(h, router_w[layer], router_b[layer], moe_w1[layer], moe_b1[layer],
                     moe_w2[layer], moe_b2[layer])
        x = x + g2 * rmsnorm(ff, norm_post_ffn[layer])
    return x


DEPTH_2 = 2

GRID_W = 64
CTX_LEN = 256
CONV_CH = 512
CONV_WIDTH = 31
N_HEADS_2 = 8
V_DIM = 2 * HEAD_DIM
QK_W = N_HEADS_2 * 2 * HEAD_DIM
ATTN_W = N_HEADS_2 * V_DIM
Q_BLOCK = 128
ROPE_BASE = 10000.0
POOL_CH = 512
POOL_WINDOWS = (2, 4, 8, 16)
POOL_GROUP = POOL_CH // len(POOL_WINDOWS)
N_BRANCH = 3
D_FF_2 = -(-(8 * D_MODEL) // (3 * 256)) * 256
N_MOD = 6
COL_A = 0
COL_Q = COL_A + 2 * CONV_CH
COL_K = COL_Q + QK_W
COL_V = COL_K + QK_W
COL_P = COL_V + ATTN_W
COL_G = COL_P + POOL_CH
IN_W = COL_G + N_BRANCH * D_MODEL


def rms_norm(x, g):
    x32 = x.astype(jnp.float32)
    y = x32 * lax.rsqrt(jnp.mean(x32 * x32, axis=-1, keepdims=True) + EPS)
    return (y * g.astype(jnp.float32)).astype(x.dtype)

def layer_norm(x, g, b):
    x32 = x.astype(jnp.float32)
    mu = jnp.mean(x32, axis=-1, keepdims=True)
    var = jnp.mean(jnp.square(x32 - mu), axis=-1, keepdims=True)
    y = (x32 - mu) * lax.rsqrt(var + EPS) * g.astype(jnp.float32) + b.astype(jnp.float32)
    return y.astype(x.dtype)

def axial_rope_tables(n_tokens):
    rows = n_tokens // GRID_W
    row = jnp.repeat(jnp.arange(rows), GRID_W).astype(jnp.float32)
    col = jnp.tile(jnp.arange(GRID_W), rows).astype(jnp.float32)
    half = HEAD_DIM // 2
    inv = ROPE_BASE ** (-jnp.arange(0, half, 2, dtype=jnp.float32) / half)
    ang_r = row[:, None] * inv[None, :]
    ang_c = col[:, None] * inv[None, :]
    return (jnp.cos(ang_r), jnp.sin(ang_r), jnp.cos(ang_c), jnp.sin(ang_c))

def _rotate(x, cos, sin):
    n = x.shape[-1] // 2
    x1, x2 = x[..., :n], x[..., n:]
    cos = cos.astype(x.dtype)
    sin = sin.astype(x.dtype)
    return jnp.concatenate([x1 * cos - x2 * sin, x2 * cos + x1 * sin], axis=-1)

def apply_axial_rope(x, rope):
    cos_r, sin_r, cos_c, sin_c = rope
    half = HEAD_DIM // 2
    return jnp.concatenate([_rotate(x[..., :half], cos_r, sin_r),
                            _rotate(x[..., half:], cos_c, sin_c)], axis=-1)

def depthwise_conv(u, w, b):
    k, ch = w.shape
    out = lax.conv_general_dilated(u, w[:, None, :].astype(u.dtype), window_strides=(1,),
                                   padding=[(k // 2, k // 2)],
                                   dimension_numbers=('NWC', 'WIO', 'NWC'),
                                   feature_group_count=ch)
    return out + b.astype(u.dtype)

def conformer_conv(h, w_glu, conv_w, conv_b, ln_g, ln_b, w_proj):
    u = h @ w_glu
    u = u[..., :CONV_CH] * jax.nn.sigmoid(u[..., CONV_CH:])
    u = depthwise_conv(u, conv_w, conv_b)
    u = layer_norm(u, ln_g, ln_b)
    return jax.nn.silu(u) @ w_proj

def multiscale_pool(h, w_p, w_group, scale, w_proj):
    p = h @ w_p
    b_, l_ = p.shape[0], p.shape[1]
    cs = jnp.cumsum(p.astype(jnp.float32), axis=1)
    cs = jnp.pad(cs, ((0, 0), (1, 0), (0, 0)))
    t = jnp.arange(l_)
    outs = []
    for gi, w in enumerate(POOL_WINDOWS):
        lo = jnp.clip(t - w // 2, 0, l_)
        hi = jnp.clip(t + w // 2, 0, l_)
        csg = cs[..., gi * POOL_GROUP:(gi + 1) * POOL_GROUP]
        s = jnp.take(csg, hi, axis=1) - jnp.take(csg, lo, axis=1)
        outs.append(s / (hi - lo).astype(jnp.float32)[None, :, None])
    pooled = jnp.concatenate(outs, axis=-1).astype(p.dtype) - p
    pooled = pooled.reshape(b_, l_, len(POOL_WINDOWS), POOL_GROUP)
    mixed = jnp.einsum('blgc,gcd->blgd', pooled, w_group).reshape(b_, l_, POOL_CH)
    return (mixed * scale) @ w_proj

def diff_qkv(h, w_q, w_k, w_v):
    b_, l_ = h.shape[0], h.shape[1]
    q = (h @ w_q).reshape(b_, l_, N_HEADS_2, 2, HEAD_DIM).transpose(0, 2, 3, 1, 4)
    k = (h @ w_k).reshape(b_, l_, N_HEADS_2, 2, HEAD_DIM).transpose(0, 2, 3, 1, 4)
    v = (h @ w_v).reshape(b_, l_, N_HEADS_2, V_DIM).transpose(0, 2, 1, 3)
    return q, k, v

def diff_attend(q, k, v, lam):
    s = jnp.einsum('bhiqd,bhikd->bhiqk', q, k).astype(jnp.float32) * (HEAD_DIM ** -0.5)
    p = jax.nn.softmax(s, axis=-1)
    a = (p[:, :, 0] - lam * p[:, :, 1]).astype(v.dtype)
    return jnp.einsum('bhqk,bhkd->bhqd', a, v)

def diff_finish(o, subln_g, lam_init, w_proj):
    o = rms_norm(o, subln_g) * (1.0 - lam_init)
    b_, h_, l_, _ = o.shape
    return o.transpose(0, 2, 1, 3).reshape(b_, l_, ATTN_W) @ w_proj

def gated_merge(h, y_a, y_b, y_c, w_g, b_gate, w_out):
    g = jax.nn.sigmoid(h @ w_g + b_gate)
    m = (g[..., :D_MODEL] * y_a + g[..., D_MODEL:2 * D_MODEL] * y_b
         + g[..., 2 * D_MODEL:] * y_c)
    return m @ w_out

def token_mixer(h, hc, rope, need_ctx, lam_init, w_in, b_gate, conv_w, conv_b, ln_g, ln_b,
                w_conv_out, lam_q1, lam_k1, lam_q2, lam_k2, subln_g, w_attn_out,
                w_pool_group, pool_scale, w_pool_out, w_out):
    w_glu = w_in[:, COL_A:COL_Q]
    w_q = w_in[:, COL_Q:COL_K]
    w_k = w_in[:, COL_K:COL_V]
    w_v = w_in[:, COL_V:COL_P]
    w_p = w_in[:, COL_P:COL_G]
    w_g = w_in[:, COL_G:IN_W]
    lam = (jnp.exp(jnp.sum(lam_q1.astype(jnp.float32) * lam_k1.astype(jnp.float32)))
           - jnp.exp(jnp.sum(lam_q2.astype(jnp.float32) * lam_k2.astype(jnp.float32)))
           + lam_init)

    qc, kc, vc = diff_qkv(hc, w_q, w_k, w_v)
    q, k, v = diff_qkv(h, w_q, w_k, w_v)
    q = apply_axial_rope(q, rope)
    k = apply_axial_rope(k, rope)
    k_all = jnp.concatenate([kc, k], axis=3)
    v_all = jnp.concatenate([vc, v], axis=2)
    b_, h_, _, l_, _ = q.shape
    nb = l_ // Q_BLOCK
    qb = jnp.moveaxis(q.reshape(b_, h_, 2, nb, Q_BLOCK, HEAD_DIM), 3, 0)
    ob = lax.map(lambda qq: diff_attend(qq, k_all, v_all, lam), qb)
    o = jnp.moveaxis(ob, 0, 2).reshape(b_, h_, l_, V_DIM)

    y_a = conformer_conv(h, w_glu, conv_w, conv_b, ln_g, ln_b, w_conv_out)
    y_b = diff_finish(o, subln_g, lam_init, w_attn_out)
    y_c = multiscale_pool(h, w_p, w_pool_group, pool_scale, w_pool_out)
    y = gated_merge(h, y_a, y_b, y_c, w_g, b_gate, w_out)
    if not need_ctx:
        return y, None
    oc = diff_attend(qc, kc, vc, lam)
    yc_a = conformer_conv(hc, w_glu, conv_w, conv_b, ln_g, ln_b, w_conv_out)
    yc_b = diff_finish(oc, subln_g, lam_init, w_attn_out)
    yc_c = multiscale_pool(hc, w_p, w_pool_group, pool_scale, w_pool_out)
    yc = gated_merge(hc, yc_a, yc_b, yc_c, w_g, b_gate, w_out)
    return y, yc

def swiglu(h, w_ffn_in, w_ffn_out):
    u = h @ w_ffn_in
    return (jax.nn.silu(u[..., :D_FF_2]) * u[..., D_FF_2:]) @ w_ffn_out

def second_inputs(seed: int = 0) -> dict:
    key = jax.random.key(seed)
    ks = jax.random.split(key, 32)
    f32 = jnp.float32
    nrm = lambda k, shape, s: jax.random.normal(k, shape, f32) * s
    gain = lambda k, shape: 1.0 + 0.02 * jax.random.normal(k, shape, f32)
    L = DEPTH_2
    return {
        "x": nrm(ks[0], (BATCH, SEQ, D_MODEL), 1.0),
        "c": nrm(ks[1], (BATCH, D_MODEL), 1.0),
        "ctx": nrm(ks[2], (BATCH, CTX_LEN, D_MODEL), 1.0),
        "c_ctx": nrm(ks[3], (D_MODEL,), 1.0),
        "w_mod": nrm(ks[4], (L, D_MODEL, N_MOD * D_MODEL), 0.5 * D_MODEL ** -0.5),
        "b_mod": nrm(ks[5], (L, N_MOD * D_MODEL), 0.02),
        "g_pre_mix": gain(ks[6], (L, D_MODEL)),
        "g_post_mix": gain(ks[7], (L, D_MODEL)),
        "w_in": nrm(ks[8], (L, D_MODEL, IN_W), D_MODEL ** -0.5),
        "b_gate": nrm(ks[9], (L, N_BRANCH * D_MODEL), 0.02),
        "conv_w": nrm(ks[10], (L, CONV_WIDTH, CONV_CH), CONV_WIDTH ** -0.5),
        "conv_b": nrm(ks[11], (L, CONV_CH), 0.02),
        "conv_ln_g": gain(ks[12], (L, CONV_CH)),
        "conv_ln_b": nrm(ks[13], (L, CONV_CH), 0.02),
        "w_conv_out": nrm(ks[14], (L, CONV_CH, D_MODEL), CONV_CH ** -0.5),
        "lam_q1": nrm(ks[15], (L, HEAD_DIM), 0.1),
        "lam_k1": nrm(ks[16], (L, HEAD_DIM), 0.1),
        "lam_q2": nrm(ks[17], (L, HEAD_DIM), 0.1),
        "lam_k2": nrm(ks[18], (L, HEAD_DIM), 0.1),
        "subln_g": gain(ks[19], (L, V_DIM)),
        "w_attn_out": nrm(ks[20], (L, ATTN_W, D_MODEL), ATTN_W ** -0.5),
        "w_pool_group": nrm(ks[21], (L, len(POOL_WINDOWS), POOL_GROUP, POOL_GROUP), POOL_GROUP ** -0.5),
        "pool_scale": 1.0 + 0.1 * jax.random.normal(ks[22], (L, POOL_CH), f32),
        "w_pool_out": nrm(ks[23], (L, POOL_CH, D_MODEL), POOL_CH ** -0.5),
        "w_out": nrm(ks[24], (L, D_MODEL, D_MODEL), D_MODEL ** -0.5),
        "g_pre_ffn": gain(ks[25], (L, D_MODEL)),
        "g_post_ffn": gain(ks[26], (L, D_MODEL)),
        "w_ffn_in": nrm(ks[27], (L, D_MODEL, 2 * D_FF_2), D_MODEL ** -0.5),
        "w_ffn_out": nrm(ks[28], (L, D_FF_2, D_MODEL), D_FF_2 ** -0.5),
    }

def second_block(x, c, ctx, c_ctx, w_mod, b_mod, g_pre_mix, g_post_mix, w_in, b_gate, conv_w,
              conv_b, conv_ln_g, conv_ln_b, w_conv_out, lam_q1, lam_k1, lam_q2, lam_k2,
              subln_g, w_attn_out, w_pool_group, pool_scale, w_pool_out, w_out, g_pre_ffn,
              g_post_ffn, w_ffn_in, w_ffn_out):
    rope = axial_rope_tables(x.shape[1])
    xl, xc = x, ctx
    for l in range(DEPTH_2):
        need_ctx = l < DEPTH_2 - 1
        lam_init = 0.8 - 0.6 * math.exp(-0.3 * l)
        mod = jax.nn.silu(c) @ w_mod[l] + b_mod[l]
        modc = jax.nn.silu(c_ctx) @ w_mod[l] + b_mod[l]
        sh1, sc1, gt1, sh2, sc2, gt2 = jnp.split(mod[:, None, :], N_MOD, axis=-1)
        csh1, csc1, cgt1, csh2, csc2, cgt2 = jnp.split(modc, N_MOD, axis=-1)

        h = rms_norm(xl, g_pre_mix[l]) * (1.0 + sc1) + sh1
        hc = rms_norm(xc, g_pre_mix[l]) * (1.0 + csc1) + csh1
        y, yc = token_mixer(h, hc, rope, need_ctx, lam_init, w_in[l], b_gate[l], conv_w[l],
                            conv_b[l], conv_ln_g[l], conv_ln_b[l], w_conv_out[l], lam_q1[l],
                            lam_k1[l], lam_q2[l], lam_k2[l], subln_g[l], w_attn_out[l],
                            w_pool_group[l], pool_scale[l], w_pool_out[l], w_out[l])
        xl = xl + gt1 * rms_norm(y, g_post_mix[l])

        h = rms_norm(xl, g_pre_ffn[l]) * (1.0 + sc2) + sh2
        xl = xl + gt2 * rms_norm(swiglu(h, w_ffn_in[l], w_ffn_out[l]), g_post_ffn[l])

        if need_ctx:
            xc = xc + cgt1 * rms_norm(yc, g_post_mix[l])
            hc = rms_norm(xc, g_pre_ffn[l]) * (1.0 + csc2) + csh2
            xc = xc + cgt2 * rms_norm(swiglu(hc, w_ffn_in[l], w_ffn_out[l]), g_post_ffn[l])
    return xl


def setup_inputs(seed=0):
    out = dict(first_inputs(seed))
    for name, value in second_inputs(seed + 1).items():
        if name != "x":
            out[name + "_2"] = value
    return out


def reference(
    x, c, w_ada, b_ada, norm_pre_mix, norm_post_mix, norm_pre_ffn, norm_post_ffn, w_in, b_in,
    conv_w, conv_b, rg_w_a, rg_b_a, rg_w_x, rg_b_x, rg_lambda, attn_sinks, w_o_rnn, w_o_attn,
    w_out, router_w, router_b, moe_w1, moe_b1, moe_w2, moe_b2, c_2, ctx_2, c_ctx_2, w_mod_2,
    b_mod_2, g_pre_mix_2, g_post_mix_2, w_in_2, b_gate_2, conv_w_2, conv_b_2, conv_ln_g_2,
    conv_ln_b_2, w_conv_out_2, lam_q1_2, lam_k1_2, lam_q2_2, lam_k2_2, subln_g_2, w_attn_out_2,
    w_pool_group_2, pool_scale_2, w_pool_out_2, w_out_2, g_pre_ffn_2, g_post_ffn_2, w_ffn_in_2,
    w_ffn_out_2,
):
    x = first_block(
        x, c, w_ada, b_ada, norm_pre_mix, norm_post_mix, norm_pre_ffn, norm_post_ffn, w_in,
        b_in, conv_w, conv_b, rg_w_a, rg_b_a, rg_w_x, rg_b_x, rg_lambda, attn_sinks, w_o_rnn,
        w_o_attn, w_out, router_w, router_b, moe_w1, moe_b1, moe_w2, moe_b2,
    )
    return second_block(
        x, c_2, ctx_2, c_ctx_2, w_mod_2, b_mod_2, g_pre_mix_2, g_post_mix_2, w_in_2, b_gate_2,
        conv_w_2, conv_b_2, conv_ln_g_2, conv_ln_b_2, w_conv_out_2, lam_q1_2, lam_k1_2,
        lam_q2_2, lam_k2_2, subln_g_2, w_attn_out_2, w_pool_group_2, pool_scale_2, w_pool_out_2,
        w_out_2, g_pre_ffn_2, g_post_ffn_2, w_ffn_in_2, w_ffn_out_2,
    )


_drawn_inputs = setup_inputs


def setup_inputs(seed=0):
    import zlib

    import numpy as np

    out = dict(_drawn_inputs(seed))
    spreads = {}
    factors = {'norm_post_ffn': 3.899,
     'rg_b_a': 8.0,
     'rg_b_x': 8.0,
     'attn_sinks': 4.13,
     'router_b': 3.161,
     'moe_b1': 7.95,
     'moe_b2': 8.0,
     'g_pre_mix_2': 6.784,
     'g_post_mix_2': 7.201,
     'b_gate_2': 8.0,
     'conv_b_2': 8.0,
     'conv_ln_g_2': 8.0,
     'conv_ln_b_2': 8.0,
     'lam_q1_2': 8.0,
     'lam_k1_2': 8.0,
     'lam_q2_2': 4.056,
     'lam_k2_2': 4.667,
     'subln_g_2': 8.0,
     'g_pre_ffn_2': 5.383,
     'g_post_ffn_2': 7.511}
    for name, (base, spread) in spreads.items():
        noise = np.random.default_rng([zlib.crc32(name.encode()), seed]).standard_normal(out[name].shape)
        drawn = base * np.exp(spread * noise) if base else spread * noise
        out[name] = __import__('jax').numpy.asarray(drawn.astype(out[name].dtype))
    for name, factor in factors.items():
        out[name] = (out[name] * factor).astype(out[name].dtype)
    return out
```

```python
import math
from contextlib import ExitStack

import numpy as np
import concourse.bass as bass
from concourse import mybir

D = 1024
KT = D // 128
S = 256
TT = 2 * S
NE = 32
DFF = 2816
FT = DFF // 128
TAPS = 31
EPS = 1e-6
LIMIT = 7.0
ALPHA = 1.702
SLOT = 64
NSLOT = 8
SLOTW = 2048
BANKS = 8
OVERMAX = 16
OVER = 3 * NE
EC = 12
OSLOT = 6
BIG = 3.0e38
FAR = 1.0e30
LAYERS = 2
HALF = FT // 2


def packed_columns():
    names = [("c", 24), ("b_ada0", 48), ("b_ada1", 48), ("b_ada2", 48),
             ("pre_mix", 8), ("post_mix", 8), ("pre_ffn", 8), ("post_ffn", 8), ("b_in", 44), ("bk", 4),
             ("conv_w", 32), ("conv_b", 8), ("b_a", 8), ("b_x", 8), ("lam", 8), ("sinks", 16)]
    for l in range(LAYERS):
        names += [(f"pre_mix{l}", 8), (f"post_mix{l}", 8), (f"pre_ffn{l}", 8), (f"post_ffn{l}", 8),
                  (f"b_gate{l}", 24), (f"taps{l}", 4 * TAPS), (f"tap_b{l}", 4), (f"ln_g{l}", 4),
                  (f"ln_b{l}", 4), (f"subln{l}", 1), (f"pool_scale{l}", 4), (f"lam_qk{l}", 4)]
    at, out = 0, {}
    for name, k in names:
        out[name] = (at, k)
        at += k
    return out, at


COLS, NCOL = packed_columns()
KEPT = {"ident": (0, 128), "rot": (128, 128), "cos": (256, S), "sin": (512, S), "edge": (768, 64)}
NKEPT = 832
ROUTE = {"slots": (0, 512), "before": (512, 128), "expert_of": (640, OVER), "round_of": (640 + OVER, OVER)}
NROUTE = 640 + 2 * OVER
NDIST = 384


def build_program(nc, a, phases="abc"):
    f32, i32 = mybir.dt.float32, mybir.dt.int32
    ALU, ACT, AX = mybir.AluOpType, mybir.ActivationFunctionType, mybir.AxisListType
    ADD, SUB, MUL, MAX, MIN, POW = ALU.add, ALU.subtract, ALU.mult, ALU.max, ALU.min, ALU.pow
    slopes = [2.0 ** (-8.0 * (h + 1) / 16) for h in range(16)]
    lam_init = [0.8 - 0.6 * math.exp(-0.3 * l) for l in range(LAYERS)]

    ctx = ExitStack()
    with ctx:
        def sb(name, width, dt=f32):
            return ctx.enter_context(nc.sbuf_tensor(name, [128, width], dt))

        def sem(name):
            return ctx.enter_context(nc.semaphore(name))

        ring = sb("ring", NSLOT * SLOTW)
        cols = sb("cols", NCOL)
        kept = sb("kept", NKEPT)
        ones = sb("ones", 128)
        ada = sb("ada", 3 * 96)
        resid = sb("resid", KT * TT)
        work = sb("work", 5 * 4096 + 6512)
        sq = sb("sq", 2 * TT)
        rs = sb("rs", 2 * TT)
        tmp = sb("tmp", TT)
        coef = sb("coef", 2 * KT)
        small = sb("small", 272)
        lists = sb("lists", 2 * OVERMAX + 1, i32)
        cstat = sb("cstat", KT * 32)
        poolw = sb("poolw", 512)
        ps = [ctx.enter_context(nc.psum_tensor(f"bank{i}", [128, 512], f32)) for i in range(BANKS)]

        def V(base, *dims):
            v = work[:, base:base + math.prod(dims)]
            if len(dims) == 2:
                return v.rearrange("p (a b) -> p a b", a=dims[0])
            if len(dims) == 3:
                return v.rearrange("p (a b c) -> p a b c", a=dims[0], b=dims[1])
            if len(dims) == 4:
                return v.rearrange("p (a b c d) -> p a b c d", a=dims[0], b=dims[1], c=dims[2])
            return v

        def C(name, i=0, n=1):
            return cols[:, COLS[name][0] + i:COLS[name][0] + i + n]

        def kept_table(name):
            at, w = KEPT[name]
            return kept[:, at:at + w]

        X = resid[:, :].rearrange("p (k t) -> p k t", k=KT)
        CS = cstat[:, :].rearrange("p (k m) -> p k m", k=KT)
        SQ = sq[:, :].rearrange("p (b t) -> p b t", b=2)
        ADA = ada[:, :].rearrange("p (n m f) -> p n m f", n=3, m=2)
        CF = coef[:, :].rearrange("p (m k) -> p m k", m=2)
        POOLW = poolw[:, :].rearrange("p (g d) -> p g d", g=4)
        CSIG = small[:, 0:24]
        SP = small[:, 24:104].rearrange("p (n k) -> p n k", n=10)
        K8, P8 = small[:, 104:112], small[:, 112:120]
        LAMP, LAME, NLAM, SUBG = small[:, 120:122], small[:, 122:124], small[:, 124:125], small[:, 125:126]
        EPSC = small[:, 134:135]
        RS = rs[:, :].rearrange("p (b t) -> p b t", b=2)
        QB = small[:, 126:134]
        ST1 = small[:, 136:152].rearrange("p (b n k) -> p b n k", b=2, n=4)
        ST = small[:, 152:216].rearrange("p (g b c n) -> p g b c n", g=2, b=2, c=2)
        GST = small[:, 216:232].rearrange("p (i n) -> p i n", i=2)
        ident, rot = kept_table("ident"), kept_table("rot")
        cos, sin = kept_table("cos"), kept_table("sin")
        edge = kept_table("edge").rearrange("p (g e) -> p g e", g=4)

        H1 = V(0, KT, S)
        XR = V(2048, KT, S + 3)
        XC = V(4120, KT, S)
        GG = V(6168, KT, S)
        GA = V(8216, KT, S)
        GI = V(10264, KT, S)
        Q1 = V(12312, KT, S)
        K1 = V(14360, 4, S)
        V1 = V(15384, 2, S)
        SR = V(15896, KT, S)
        SA = V(17944, KT, S)
        BD = V(19992, 2, KT, 128)
        MU = V(22040, KT, S)
        P1 = V(24088, 2, NDIST)
        PT1 = V(24856, 2, NDIST)
        DIST = V(25624, NDIST)
        ROWS = V(26008, S + NE)
        M1 = V(2048, KT, S)
        MX1 = H1
        ADR = V(22040, 3, 512)
        H2 = V(0, KT, S)
        HT = V(2048, 2, D)
        FF = V(4096, KT, S)
        B1 = V(6144, 2 * D)
        XE = V(8192, KT, SLOT)
        PSEL = V(8704, 2, 128)
        GSEL = V(8960, 2, 128)
        PGT = V(9216, 2, S)
        GLU, SIG, LIN, AC = (V(9728 + 512 * i, 512) for i in range(4))
        AT = V(11776, 4, 128)
        YE = V(12288, 512)
        B2 = V(12800, D)
        RW = V(13824, KT, NE)
        LG = V(14080, 2, NE + 8)
        LR = V(14160, 2, NE + 8)
        MK = V(14240, 2, NE)
        GATE = V(14304, 2, NE + 2)
        POS = V(14372, 2, NE + 2)
        EX = V(14440, 2, NE)
        BSEL = V(14504, 2, SLOT)
        GATET = V(14632, S)
        M8 = V(14888, 2, 16)
        OFLAG = V(14920, OVER)
        OCUM = V(15016, OVER)
        OEXP = V(15112, OVER)
        ORND = V(15208, OVER)
        OJUNK = V(15304, OVER)
        OLIST = V(15400, 2 * OVERMAX)
        RT = V(15448, NROUTE)

        def route_table(name):
            at, w = ROUTE[name]
            return RT[:, at:at + w]

        before = route_table("before")
        H = V(0, KT, TT)
        M = V(4096, KT, TT)
        Q = V(8192, KT, TT)
        K = V(12288, KT, TT)
        VV = V(16384, 4, D)
        U = V(20480, 4, 2, S + TAPS - 1)
        UC = V(22768, 4, TT)
        PL = V(24816, 4, 2, S + 16)
        PR = V(4096, 2, 2, 2, 512)
        AT2 = V(20480, 2, 4, S)
        GR = V(12288, 4, TT)
        PA = V(14336, 2, S + 16)
        PB = V(14880, 2, S + 16)
        PO = V(16384, 4, TT)
        FA = V(8192, FT, TT)

        consts_in, x_in, rows_in, dist_in = (sem(n) for n in ("consts_in", "x_in", "rows_in", "dist_in"))
        moe_consts_in, poolw_in, out_written, bd_in = (
            sem(n) for n in ("moe_consts_in", "poolw_in", "out_written", "bd_in"))
        chunk_full = [sem(f"chunk_full{s}") for s in range(NSLOT)]
        chunk_part_read = sem("chunk_part_read")
        pe_job = sem("pe_job")
        bank_free = [sem(f"bank_free{b}") for b in range(BANKS)]
        dve_chain, act_chain, pool_chain = sem("dve_chain"), sem("act_chain"), sem("pool_chain")
        ones_set, bd_zeroed, silu_sig, silu_set = (sem(n) for n in ("ones_set", "bd_zeroed", "silu_sig", "silu_set"))
        ada_set, squared, scaled, h_set, x_set = (
            sem(n) for n in ("ada_set", "squared", "scaled", "h_set", "x_set"))
        sp_abs, sp_exp, sp_one, sp_ln, sp_set = (sem(n) for n in ("sp_abs", "sp_exp", "sp_one", "sp_ln", "sp_set"))
        q_bias_set, conv1_set, decay_set, rnn_set = (
            sem(n) for n in ("q_bias_set", "conv1_set", "decay_set", "rnn_set"))
        max_set, prob_set, prob_normed, merged = (
            sem(n) for n in ("max_set", "prob_set", "prob_normed", "merged"))
        rmax_set, rexp_set, gate_set, mask_set, pos_set, lists_set, ff_done = (
            sem(n) for n in ("rmax_set", "rexp_set", "gate_set", "mask_set", "pos_set", "lists_set", "ff_done"))
        moe_full = [sem(f"moe_full{s}") for s in range(NSLOT)]
        over_full = [sem(f"over_full{s}") for s in range(OSLOT)]
        moe_read = sem("moe_read")
        gathered, gate_turned, act_turned, scattered = (
            sem(n) for n in ("gathered", "gate_turned", "act_turned", "scattered"))
        sel_set, glu_set, lin_set, half_act, act_set, added0, added1 = (
            sem(n) for n in ("sel_set", "glu_set", "lin_set", "half_act", "act_set", "added0", "added1"))
        xe_set, pgt_set, sig_set, at_set, ye_set = (
            sem(n) for n in ("xe_set", "pgt_set", "sig_set", "at_set", "ye_set"))
        lam_prod, rotated, heads_normed, centred, conv_scaled, conv_act, pooled = (
            sem(n) for n in ("lam_prod", "rotated", "heads_normed", "centred", "conv_scaled", "conv_act", "pooled"))
        eps_set, mult_sq, mult_set = sem("eps_set"), sem("mult_sq"), sem("mult_set")
        b1_zeroed = sem("b1_zeroed")

        rms_buffer = {}
        moe_base = []
        jobs = {}
        chunks = []
        release = []
        sq_release = []
        counts = {}

        def count(s, k=1):
            counts[id(s)] = counts.get(id(s), 0) + k
            return counts[id(s)]

        def bank(name):
            return ps[jobs[name] % BANKS]

        def job_done(eng, name):
            eng.wait_ge(pe_job, jobs[name] + 1)

        def bank_signal(name):
            return bank_free[jobs[name] % BANKS], jobs[name] // BANKS + 1

        def evacuated(eng, name):
            s, v = bank_signal(name)
            eng.wait_ge(s, v)

        def parts_of(lo):
            return [(0, S, 1), (S, TT, 0)] if lo == 0 else [(S, TT, 0)]

        def segments(ap):
            return ap.rearrange("p (s t) -> p s t", t=S)

        def groups_of(l):
            return [g for hd in range(8) for g in (([(hd, (0, 1), S)] if l == 0 else []) + [(hd, (2, 3), TT)])]

        class Next:

            def __init__(self, eng):
                self.eng, self.n = eng, {}

            def __call__(self, s, k=1):
                self.n[id(s)] = self.n.get(id(s), 0) + k
                self.eng.wait_ge(s, self.n[id(s)])

        block = ctx.enter_context(nc.Block())

        @block.tensor
        def _(pe):
            full = [0] * NSLOT

            def open_job(name):
                n = len(jobs)
                jobs[name] = n
                if n >= BANKS:
                    pe.wait_ge(bank_free[n % BANKS], n // BANKS)
                return ps[n % BANKS]

            def take_chunk(*loads):
                s = len(chunks) % NSLOT
                chunks.append(loads)
                release.append(None)
                full[s] += 16 * len(loads)
                pe.wait_ge(chunk_full[s], full[s])
                return ring[:, s * SLOTW:(s + 1) * SLOTW]

            def chunk_read_with_job(i=-1):
                release[i] = (pe_job, len(jobs))

            def chunk_read_inside(mm):
                mm.then_inc(chunk_part_read, 1)
                release[-1] = (chunk_part_read, count(chunk_part_read))

            def tiles(w_ap, c0, n=2, rows=D):
                return w_ap[:, c0:c0 + 128 * n].rearrange("(k p) n -> p k n", p=128), rows * n

            def linear(names, w, kt, rhs):
                wv = w[:, 0:kt * 128 * len(names)].rearrange("p (k n) -> p k n", k=kt)
                for i, name in enumerate(names):
                    o = open_job(name)
                    for k in range(kt):
                        mm = pe.matmul(o[:, 0:rhs(k).shape[-1]], wv[:, k, i * 128:(i + 1) * 128], rhs(k),
                                       start=(k == 0), stop=(k == kt - 1))
                    mm.then_inc(pe_job, 1)
                chunk_read_with_job()

            def modulation(n, w_ap):
                for q in range(3):
                    o = open_job(f"ada{n}.{q}")
                    for k in range(KT):
                        w = take_chunk((w_ap[k * 128:(k + 1) * 128, q * SLOTW:(q + 1) * SLOTW], SLOTW))
                        for j in range(4):
                            mm = pe.matmul(o[32 * j:32 * j + 32, :], CS[:, k, :], w[:, j * 512:(j + 1) * 512],
                                           start=(k == 0), stop=(k == KT - 1))
                        if k < KT - 1:
                            chunk_read_inside(mm)
                    mm.then_inc(pe_job, 1)
                    chunk_read_with_job()
                for q in range(3):
                    evacuated(pe, f"ada{n}.{q}")
                    o = open_job(f"adaT{n}.{q}")
                    for s in range(4):
                        mm = pe.transpose(o[:, s * 128:(s + 1) * 128], ADR[:, q, s * 128:(s + 1) * 128], ident)
                    mm.then_inc(pe_job, 1)

            def square_sum(name, n, width):
                o = open_job(name)
                for t in range(n):
                    m = len(sq_release)
                    pe.wait_ge(squared, m + 1)
                    mm = pe.matmul(o[:, 0:width], ones[:, :], SQ[:, m % 2, 0:width], start=(t == 0), stop=(t == n - 1))
                    if t < n - 1:
                        mm.then_inc(chunk_part_read, 1)
                        sq_release.append((chunk_part_read, count(chunk_part_read)))
                mm.then_inc(pe_job, 1)
                sq_release.append((pe_job, len(jobs)))
                rms_buffer[name] = len(rms_buffer) % 2

            def block1():
                square_sum("b1.pre", KT, S)
                modulation(0, a["w_ada"])
                pe.wait_ge(h_set, KT)

                def h(k):
                    return H1[:, k, :]

                for part, c0, n in (("xr", 0, 4), ("gr", 1024, 4), ("q", 2048, 4)):
                    for c in range(n):
                        w = take_chunk(tiles(a["w_in"], c0 + 256 * c))
                        linear([f"{part}{2 * c}", f"{part}{2 * c + 1}"], w, KT, h)
                w = take_chunk(tiles(a["w_in"], 3072))
                wv = w.rearrange("p (k n) -> p k n", k=KT)
                for g in range(4):
                    o = open_job(f"k{g}")
                    for k in range(KT):
                        for p0 in (0, 64):
                            mm = pe.matmul(o[p0:p0 + 64, 0:S], wv[:, k, 64 * g:64 * g + 64],
                                           H1[:, k, :], start=(k == 0), stop=(k == KT - 1))
                    mm.then_inc(pe_job, 1)
                chunk_read_with_job()
                w = take_chunk(tiles(a["w_in"], 3328))
                wv = w.rearrange("p (k n) -> p k n", k=KT)
                pe.wait_ge(rows_in, 16)
                for i in range(2):
                    o = open_job(f"v{i}")
                    for k in range(KT):
                        pe.matmul(o[:, 0:256], H1[:, k, 128 * i:128 * i + 128], wv[:, k, :],
                                  start=(k == 0), stop=False)
                    pe.matmul(o[:, 0:256], ones[0:1, :], ROWS[0:1, 0:256], start=False, stop=True)\
                        .then_inc(pe_job, 1)
                chunk_read_with_job()
                for part, c0 in (("sr", 3584), ("sa", 4608)):
                    for c in range(4):
                        w = take_chunk(tiles(a["w_in"], c0 + 256 * c))
                        linear([f"{part}{2 * c}", f"{part}{2 * c + 1}"], w, KT, h)
                pe.wait_ge(bd_in, 64)
                pe.wait_ge(conv1_set, 1)
                for part, b in (("ga", 0), ("gi", 1)):
                    for t in range(KT):
                        o = open_job(f"{part}{t}")
                        pe.matmul(o[:, 0:S], BD[:, b, t, :], XC[:, t, :], start=True, stop=True)\
                            .then_inc(pe_job, 1)
                evacuated(pe, "q7")
                evacuated(pe, "k3")
                evacuated(pe, "v1")

                def scores(hd):
                    p0, t, g = 64 * (hd % 2), hd // 2, hd // 4
                    o = open_job(f"s{hd}")
                    pe.matmul(o[:, 0:128], Q1[p0:p0 + 64, t, 0:128], K1[p0:p0 + 64, g, 0:128], start=True, stop=True)
                    pe.matmul(o[:, 128:384], Q1[p0:p0 + 64, t, 128:256], K1[p0:p0 + 64, g, :], start=True, stop=True)\
                        .then_inc(pe_job, 1)

                scores(0)
                for hd in range(16):
                    if hd < 15:
                        scores(hd + 1)
                    p0, g = 64 * (hd % 2), hd // 4
                    pe.wait_ge(prob_normed, hd + 1)
                    o = open_job(f"pt{hd}")
                    for j in range(3):
                        mm = pe.transpose(o[:, j * 128:(j + 1) * 128], P1[:, hd % 2, j * 128:(j + 1) * 128], ident)
                    mm.then_inc(pe_job, 1)
                    evacuated(pe, f"pt{hd}")
                    o = open_job(f"o{hd}")[p0:p0 + 64, :]
                    pe.matmul(o[:, 0:128], V1[:, 0, 64 * g:64 * g + 64], PT1[:, hd % 2, 0:128], start=True, stop=True)
                    for j in range(2):
                        mm = pe.matmul(o[:, 128:256], V1[:, j, 64 * g:64 * g + 64],
                                       PT1[:, hd % 2, 128 * (j + 1):128 * (j + 2)], start=(j == 0), stop=(j == 1))
                    mm.then_inc(pe_job, 1)
                pe.wait_ge(rnn_set, 1)
                evacuated(pe, "o15")
                evacuated(pe, "o14")
                for c in range(4):
                    w = take_chunk(tiles(a["w_o_rnn"], 256 * c))
                    linear([f"yr{2 * c}", f"yr{2 * c + 1}"], w, KT, lambda k: GG[:, k, :])
                    w = take_chunk(tiles(a["w_o_attn"], 256 * c))
                    linear([f"ya{2 * c}", f"ya{2 * c + 1}"], w, KT, lambda k: Q1[:, k, :])
                pe.wait_ge(merged, KT)
                for c in range(4):
                    w = take_chunk(tiles(a["w_out"], 256 * c))
                    linear([f"mx{2 * c}", f"mx{2 * c + 1}"], w, KT, lambda k: M1[:, k, :])
                square_sum("b1.post", KT, S)
                square_sum("b1.ffn", KT, S)

            def gather(gi, par):
                pe.wait_ge(sel_set, gi[0])
                for ft in range(KT):
                    for i in range(2):
                        mm = pe.matmul(ps[2][:, ft * SLOT:(ft + 1) * SLOT], HT[:, i, ft * 128:(ft + 1) * 128],
                                       PSEL[:, i, 0:SLOT], start=(i == 0), stop=(i == 1))
                mm.then_inc(gathered, 1)
                for i in range(2):
                    mm = pe.transpose(ps[3][:, i * 128:(i + 1) * 128], GSEL[:, i, :], ident)
                mm.then_inc(gate_turned, 1)

            def hidden(n, gi, par, slot_of, full_wait):
                pe.wait_ge(xe_set, gi + 1)
                pe.wait_ge(pgt_set, gi + 1)
                pe.wait_ge(added0, n)
                for b in range(2):
                    for p0 in (0, 64):
                        c0 = D * (p0 // 64) + 512 * b
                        pe.matmul(ps[b][p0:p0 + 64, :], BSEL[:, par, :], B1[:, c0:c0 + 512], start=True, stop=False)
                for k in range(KT):
                    full_wait(k)
                    w = ring[:, slot_of(k) * SLOTW:(slot_of(k) + 1) * SLOTW]
                    for b in range(2):
                        for p0 in (0, 64):
                            c0 = D * (p0 // 64) + 512 * b
                            mm = pe.matmul(ps[b][p0:p0 + 64, :], XE[:, k, :], w[:, c0:c0 + 512],
                                           start=False, stop=(k == KT - 1))
                    mm.then_inc(moe_read, 1)

            def down(n, par, slot_of, full_wait):
                pe.wait_ge(act_set, n + 1)
                for j in range(4):
                    mm = pe.transpose(ps[4][:, j * 128:(j + 1) * 128], AC[:, j * 128:(j + 1) * 128], ident)
                mm.then_inc(act_turned, 1)
                pe.wait_ge(at_set, n + 1)
                for k in range(KT):
                    c = KT + k // 2
                    if k % 2 == 0:
                        full_wait(c)
                    w = ring[:, slot_of(c) * SLOTW + D * (k % 2):slot_of(c) * SLOTW + D * (k % 2) + D]
                    for p0 in (0, 64):
                        c0 = 512 * (p0 // 64)
                        mm = pe.matmul(ps[5][p0:p0 + 64, :], AT[:, k % 4, 64 * (k // 4):64 * (k // 4) + 64],
                                       w[:, c0:c0 + 512], start=(k == 0), stop=(k == KT - 1))
                    if k % 2:
                        mm.then_inc(moe_read, 1)

            def scatter(n, gi, par):
                pe.wait_ge(ye_set, n + 1)
                for r in range(2):
                    if r:
                        pe.wait_ge(added1, n)
                    for f in range(2):
                        for half, p0 in enumerate((0, 64)):
                            mm = pe.matmul(ps[(0, 6)[r] + half][:, f * S:(f + 1) * S],
                                           YE[p0:p0 + 64, (2 * r + f) * 128:(2 * r + f + 1) * 128],
                                           PGT[p0:p0 + 64, par, :], start=True, stop=True)
                    mm.then_inc(scattered, 1)

            def moe():
                pe.wait_ge(moe_consts_in, 16 * 4)
                pe.wait_ge(h_set, 2 * KT)
                for i in range(2):
                    o = open_job(f"lg{i}")
                    for k in range(KT):
                        pe.matmul(o[:, 0:NE], H2[:, k, 128 * i:128 * i + 128], RW[:, k, :], start=(k == 0), stop=False)
                    pe.matmul(o[:, 0:NE], ones[0:1, :], ROWS[0:1, S:S + NE], start=False, stop=True)\
                        .then_inc(pe_job, 1)
                for i in range(2):
                    for half in range(2):
                        o = open_job(f"ht{i}{half}")
                        for j in range(4):
                            mm = pe.transpose(o[:, j * 128:(j + 1) * 128],
                                              H2[:, 4 * half + j, 128 * i:128 * i + 128], ident)
                        mm.then_inc(pe_job, 1)
                modulation(1, a["w_mod_2"][0])
                pe.wait_ge(mask_set, 2)
                for i in range(2):
                    o = open_job(f"pos{i}")
                    if i:
                        pe.matmul(o[:, 0:NE], ones[:, :], MK[:, 0, :], start=True, stop=False)
                    pe.matmul(o[:, 0:NE], before, MK[:, i, :], start=(i == 0), stop=True).then_inc(pe_job, 1)
                o = open_job("cnt")
                for i in range(2):
                    mm = pe.matmul(o[:, 0:NE], ones[:, :], MK[:, i, :], start=(i == 0), stop=(i == 1))
                mm.then_inc(pe_job, 1)
                pe.wait_ge(gate_set, 2)
                o = open_job("gt")
                for i in range(2):
                    mm = pe.transpose(o[0:NE, i * 128:(i + 1) * 128], GATE[:, i, 0:NE], ident)
                mm.then_inc(pe_job, 1)
                evacuated(pe, "gt")
                for j in range(4):
                    o = open_job(f"b2{j}")
                    for f in range(2):
                        mm = pe.matmul(o[:, f * S:(f + 1) * S], B2[0:NE, (2 * j + f) * 128:(2 * j + f + 1) * 128],
                                       GATET[0:NE, :], start=True, stop=True)
                    mm.then_inc(pe_job, 1)
                for name in list(jobs)[-BANKS:]:
                    evacuated(pe, name)
                base = len(chunks)
                gather([1], 0)
                with pe.Fori(0, NE // 2) as it:
                    for u in range(2):
                        n = it * 2 + u

                        def full_wait(c, it=it, u=u):
                            j = EC * u + c
                            pe.wait_ge(moe_full[(base + j) % NSLOT], it * 48 + 16 * (j // NSLOT + 1))

                        def slot_of(c, u=u):
                            return (base + EC * u + c) % NSLOT

                        hidden(n, n, u, slot_of, full_wait)
                        gather([n + 2], 1 - u)
                        down(n, u, slot_of, full_wait)
                        scatter(n, n, u)
                moe_base.append(base)
                pe.wait_ge(lists_set, 1)
                n_over = pe.value_load(lists[0:1, 2 * OVERMAX:2 * OVERMAX + 1], min_val=0, max_val=OVERMAX)
                with pe.If(n_over > 0):
                    with pe.Fori(0, n_over) as q:
                        n = q + NE

                        def full_wait(c, q=q):
                            pe.wait_ge(over_full[c % OSLOT], q * 32 + 16 * (c // OSLOT + 1))

                        gather([q + (NE + 3)], 0)
                        hidden(n, q + (NE + 1), 0, lambda c: c % OSLOT, full_wait)
                        down(n, 0, lambda c: c % OSLOT, full_wait)
                        scatter(n, q + (NE + 1), 0)
                with pe.Else():
                    pass
                square_sum("b1.out", KT, S)

            def layer(l):
                lo = 0 if l == 0 else S
                w_in = a["w_in_2"][l]
                width = TT - lo
                square_sum(f"pre{l}", KT, TT)
                pe.wait_ge(h_set, KT * (2 + 2 * l + 1))

                def h(k):
                    return H[:, k, lo:TT]

                def h_all(k):
                    return H[:, k, :]

                for c in range(2):
                    for part, c0 in (("lg", 512), ("la", 0)):
                        w = take_chunk(tiles(w_in, c0 + 256 * c))
                        linear([f"{part}{l}.{2 * c}", f"{part}{l}.{2 * c + 1}"], w, KT, h)
                for part, c0, rhs in (("q", 1024, h), ("k", 2048, h_all)):
                    for c in range(4):
                        w = take_chunk(tiles(w_in, c0 + 256 * c))
                        linear([f"{part}{l}.{2 * c}", f"{part}{l}.{2 * c + 1}"], w, KT, rhs)
                for c in range(4):
                    w = take_chunk(tiles(w_in, 3072 + 256 * c))
                    wv = w.rearrange("p (k n) -> p k n", k=KT)
                    for i in range(0, 4, 2):
                        o = open_job(f"v{l}.{c}.{i}")
                        for ii in range(2):
                            for k in range(KT):
                                mm = pe.matmul(o[:, ii * 256:ii * 256 + 256],
                                               H[:, k, (i + ii) * 128:(i + ii + 1) * 128], wv[:, k, :],
                                               start=(k == 0), stop=(k == KT - 1))
                        mm.then_inc(pe_job, 1)
                    chunk_read_with_job()
                for t in range(KT):
                    for part, view in (("q", Q), ("k", K)):
                        evacuated(pe, f"{part}{l}.{t}")
                        o = open_job(f"rot{part}{l}.{t}")
                        pe.matmul(o[:, 0:S], rot, view[:, t, S:TT], start=True, stop=True).then_inc(pe_job, 1)
                for c in range(2):
                    w = take_chunk(tiles(w_in, 4096 + 256 * c))
                    linear([f"p{l}.{2 * c}", f"p{l}.{2 * c + 1}"], w, KT, h)
                o = open_job(f"lam{l}")
                pe.wait_ge(lam_prod, l + 1)
                pe.matmul(o[:, 0:2], ones[:, :], LAMP, start=True, stop=True).then_inc(pe_job, 1)

                groups = groups_of(l)

                def scores(gi):
                    hd, blocks, nk = groups[gi]
                    if gi == 0:
                        pe.wait_ge(rotated, l + 1)
                    for b in blocks:
                        for comp in range(2):
                            o = open_job(f"s{l}.{gi}.{b}.{comp}")
                            pe.matmul(o[:, 0:nk], Q[64 * comp:64 * comp + 64, hd, b * 128:(b + 1) * 128],
                                      K[64 * comp:64 * comp + 64, hd, 0:nk], start=True, stop=True)\
                                .then_inc(pe_job, 1)

                scores(0)
                for gi, (hd, blocks, nk) in enumerate(groups):
                    if gi + 1 < len(groups):
                        scores(gi + 1)
                    for j, b in enumerate(blocks):
                        pe.wait_ge(prob_normed, 16 + 32 * l + 2 * gi + j + 1)
                        o = open_job(f"pt{l}.{gi}.{b}")
                        for k in range(nk // 128):
                            mm = pe.transpose(o[:, k * 128:(k + 1) * 128],
                                              PR[:, gi % 2, j, 0, k * 128:(k + 1) * 128], ident)
                        mm.then_inc(pe_job, 1)
                    for b in blocks:
                        evacuated(pe, f"pt{l}.{gi}.{b}")
                    o = open_job(f"o{l}.{gi}")
                    for k in range(nk // 128):
                        mm = pe.matmul(o[:, 0:S], VV[:, k, hd * 128:(hd + 1) * 128], AT2[:, gi % 2, k, :],
                                       start=(k == 0), stop=(k == nk // 128 - 1))
                    mm.then_inc(pe_job, 1)
                for hd in range(KT):
                    square_sum(f"sub{l}.{hd}", 1, width)
                o = open_job(f"mean{l}")
                for t in range(4):
                    mm = pe.matmul(o[:, 0:width], ones[:, :], UC[:, t, lo:TT], start=(t == 0), stop=(t == 3))
                mm.then_inc(pe_job, 1)
                square_sum(f"var{l}", 4, width)
                pe.wait_ge(poolw_in, 16 * (l + 1))
                for t in range(4):
                    pe.wait_ge(pooled, 4 * l + t + 1)
                    o = open_job(f"pm{l}.{t}")
                    pe.matmul(o[:, 0:width], POOLW[:, t, :], PO[:, t, lo:TT], start=True, stop=True)\
                        .then_inc(pe_job, 1)

                def gates(br, c):
                    w = take_chunk(tiles(w_in, 4608 + D * br + 256 * c))
                    linear([f"g{l}.{br}.{2 * c}", f"g{l}.{br}.{2 * c + 1}"], w, KT, h)

                for br, wy, src in ((0, "w_conv_out_2", UC), (1, "w_attn_out_2", Q), (2, "w_pool_out_2", PO)):
                    if br == 1:
                        for c in range(4):
                            gates(1, c)
                            w = take_chunk(tiles(a[wy][l], 256 * c))
                            if c == 0:
                                pe.wait_ge(heads_normed, KT * (l + 1))
                            linear([f"y{l}.1.{2 * c}", f"y{l}.1.{2 * c + 1}"], w, KT, lambda k: Q[:, k, lo:TT])
                        continue
                    for c in range(2):
                        gates(br, 2 * c)
                        gates(br, 2 * c + 1)
                        w = take_chunk(tiles(a[wy][l], 512 * c, 4, 512))
                        if c == 0 and br == 0:
                            pe.wait_ge(conv_act, 4 * (l + 1))
                        if c == 0 and br == 2:
                            for t in range(4):
                                evacuated(pe, f"pm{l}.{t}")
                        linear([f"y{l}.{br}.{4 * c + i}" for i in range(4)], w, 4,
                               lambda k, src=src: src[:, k, lo:TT])
                pe.wait_ge(merged, KT * (l + 2))
                for c in range(4):
                    w = take_chunk(tiles(a["w_out_2"][l], 256 * c))
                    linear([f"m{l}.{2 * c}", f"m{l}.{2 * c + 1}"], w, KT, lambda k: M[:, k, lo:TT])
                square_sum(f"post{l}", KT, width)
                if l == 0:
                    modulation(2, a["w_mod_2"][1])
                square_sum(f"ffn{l}", KT, width)
                pe.wait_ge(h_set, KT * (2 + 2 * l + 2))
                w1 = a["w_ffn_in_2"][l]
                for c in range(HALF):
                    for part, c0 in (("fg", 0), ("fu", DFF)):
                        w = take_chunk(tiles(w1, c0 + 256 * c))
                        linear([f"{part}{l}.{2 * c}", f"{part}{l}.{2 * c + 1}"], w, KT, h)
                evacuated(pe, f"fu{l}.{FT - 2}")
                evacuated(pe, f"fu{l}.{FT - 1}")
                w2 = a["w_ffn_out_2"][l]
                for t in range(KT):
                    o = open_job(f"f{l}.{t}")
                    for half in range(2):
                        src = w2[half * HALF * 128:(half + 1) * HALF * 128, t * 128:(t + 1) * 128]
                        w = take_chunk((src.rearrange("(k p) n -> p k n", p=128), HALF * 128))
                        wv = w[:, 0:HALF * 128].rearrange("p (k n) -> p k n", k=HALF)
                        for k in range(HALF):
                            mm = pe.matmul(o[:, 0:width], wv[:, k, :], FA[:, half * HALF + k, lo:TT],
                                           start=(half == 0 and k == 0), stop=(half == 1 and k == HALF - 1))
                        if half == 0:
                            chunk_read_inside(mm)
                    mm.then_inc(pe_job, 1)
                    chunk_read_with_job()
                square_sum(f"out{l}", KT, width)

            pe.wait_ge(ones_set, 1)
            pe.wait_ge(consts_in, 32)
            pe.wait_ge(silu_set, 1)
            if "a" in phases:
                block1()
            if "b" in phases:
                moe()
            if "c" in phases:
                for l in range(LAYERS):
                    layer(l)


        @block.sync
        def _(sp):
            sp.dma_start(cols[:, :], a["cols"]).then_inc(consts_in, 16)
            sp.dma_start(kept[:, :], a["kept"]).then_inc(consts_in, 16)
            sp.dma_start(X[:, :, S:TT], a["x"].rearrange("(k p) t -> p k t", p=128)).then_inc(x_in, 16)

            def slot_view(s, src, at, n):
                v = ring[:, s * SLOTW + at:s * SLOTW + at + n]
                return v.rearrange("p (k n) -> p k n", k=src.shape[1]) if len(src.shape) == 3 else v

            def ordinary(c, n_over=0):
                if c >= NSLOT:
                    if moe_base and moe_base[0] <= c < moe_base[0] + NSLOT:
                        last = EC * NE - NSLOT + (c - moe_base[0]) + 1
                        s = c % NSLOT
                        if s < OSLOT:
                            sp.wait_ge(moe_read, n_over * EC + max(last, EC * (NE - 1) + OSLOT + s + 1))
                        else:
                            sp.wait_ge(moe_read, last)
                    else:
                        s, v = release[c - NSLOT]
                        sp.wait_ge(s, v)
                at = 0
                for src, n in chunks[c]:
                    sp.dma_start(slot_view(c % NSLOT, src, at, n), src).then_inc(chunk_full[c % NSLOT], 16)
                    at += n

            def expert_chunk(e, c):
                if c < KT:
                    return a["moe_w1"][bass.ds(e, 1), c * 128:(c + 1) * 128, :].rearrange("a p n -> p (a n)")
                r = (c - KT) * 256
                return a["moe_w2"][bass.ds(e, 1), r:r + 256, :].rearrange("a (k p) n -> p (a k) n", p=128)

            def load_expert(e, c, s, full):
                src = expert_chunk(e, c)
                sp.dma_start(slot_view(s, src, 0, SLOTW), src).then_inc(full, 16)

            n_over = 0
            n_before = moe_base[0] if moe_base else len(chunks)
            for c in range(n_before):
                ordinary(c)
                if c == 8:
                    sp.dma_start(X[:, :, 0:S], a["ctx"].rearrange("(k p) t -> p k t", p=128)).then_inc(x_in, 16)
            if moe_base:
                base = moe_base[0]

                def load(it, g):
                    s = (base + g) % NSLOT
                    load_expert(it * 2 + g // EC, g % EC, s, moe_full[s])

                for g in range(NSLOT):
                    s, v = release[base + g - NSLOT]
                    sp.wait_ge(s, v)
                    load(0, g)
                with sp.Fori(0, NE // 2 - 1) as it:
                    for m in range(2 * EC):
                        sp.wait_ge(moe_read, it * (2 * EC) + m + 1)
                        load(it, NSLOT + m)
                for m in range(2 * EC - NSLOT):
                    sp.wait_ge(moe_read, (NE // 2 - 1) * 2 * EC + m + 1)
                    load(NE // 2 - 1, NSLOT + m)
                sp.wait_ge(lists_set, 1)
                n_over = sp.value_load(lists[0:1, 2 * OVERMAX:2 * OVERMAX + 1], min_val=0, max_val=OVERMAX)
                with sp.If(n_over > 0):
                    sp.wait_ge(moe_read, EC * NE)
                    with sp.Fori(0, n_over) as q:
                        e = sp.value_load(lists[0:1, bass.ds(q, 1)], min_val=0, max_val=NE - 1)
                        for c in range(EC):
                            sp.wait_ge(moe_read, q * EC + (EC * NE - OSLOT + c + 1))
                            load_expert(e, c, c % OSLOT, over_full[c % OSLOT])
                with sp.Else():
                    pass
            for c in range(n_before, len(chunks)):
                ordinary(c, n_over)
            out_t = a["out"].rearrange("(k p) t -> p k t", p=128)
            sp.wait_ge(x_set, KT * (("a" in phases) + ("b" in phases) + 2 * LAYERS * ("c" in phases)))
            sp.dma_start(out_t, X[:, :, S:TT]).then_inc(out_written, 16)
            sp.wait_ge(out_written, 16)

        @block.gpsimd
        def _(pool):
            chain = [0]

            def link(ins):
                chain[0] += 1
                ins.then_inc(pool_chain, 1)
                pool.wait_ge(pool_chain, chain[0])

            pool.memset(ones[:, :], 1.0).then_inc(ones_set, 1)
            pool.memset(V(19992, 2 * KT * 128), 0.0).then_inc(bd_zeroed, 1)
            pool.dma_start(ROWS[0:1, :], a["rows"]).then_inc(rows_in, 16)
            pool.dma_start(DIST, a["dist"]).then_inc(dist_in, 16)
            pool.wait_ge(bd_zeroed, 1)
            for b, name in enumerate(("rg_w_a", "rg_w_x")):
                w = a[name].rearrange("(t h) i j -> h i t j", h=2)
                for half in range(2):
                    pool.dma_start(BD[64 * half:64 * half + 64, b, :, 64 * half:64 * half + 64], w[half])\
                        .then_inc(bd_in, 16)
            if "b" in phases:
                if "a" in phases:
                    job_done(pool, "ya7")
                pool.memset(B1, 0.0).then_inc(b1_zeroed, 1)
                pool.dma_start(B2[0:NE, :], a["moe_b2"]).then_inc(moe_consts_in, 16)
                pool.dma_start(RW, a["router_w"].rearrange("(k p) e -> p k e", p=128)).then_inc(moe_consts_in, 16)
                pool.dma_start(RT, a["route"]).then_inc(moe_consts_in, 16)
                pool.wait_ge(b1_zeroed, 1)
                pool.dma_start(B1[0:NE, :], a["moe_b1"]).then_inc(moe_consts_in, 16)
            if "c" in phases:
                for l in range(LAYERS):
                    if l:
                        job_done(pool, f"pm{l - 1}.3")
                    pool.dma_start(POOLW, a["w_pool_group_2"][l].rearrange("g c d -> c g d")).then_inc(poolw_in, 16)
                    lo = 0 if l == 0 else S
                    s0 = lo // S
                    job_done(pool, f"pre{l}")
                    link(pool.memset(PL[:, :, :, 0:8], 0.0))
                    link(pool.memset(PL[:, :, :, S + 8:S + 16], 0.0))
                    job_done(pool, f"o{l}.{len(groups_of(l)) - 1}")
                    for g in range(4):
                        evacuated(pool, f"p{l}.{g}")
                        src = PL[:, g, s0:2, :]
                        n = S + 16
                        for i in range(g + 1):
                            dst = (PA, PB)[i % 2][:, s0:2, :]
                            n -= 1 << i
                            link(pool.tensor_tensor(dst[:, :, 0:n], src[:, :, 0:n], src[:, :, 1 << i:n + (1 << i)], ADD))
                            src = dst
                        w = 2 << g
                        out = segments(PO[:, g, lo:TT])
                        link(pool.tensor_scalar(out, src[:, :, 8 - w // 2:8 - w // 2 + S], 1.0 / w, None, MUL))
                        for e0, c0 in ((0, 0), (8, S - 8)):
                            for s in range(2 - s0):
                                v = out[:, s, c0:c0 + 8]
                                link(pool.tensor_tensor(v, v, edge[:, g, e0:e0 + 8], MUL))
                        pool.tensor_tensor(out, out, PL[:, g, s0:2, 8:8 + S], SUB).then_inc(pooled, 1)
                        pool.wait_ge(pooled, count(pooled))

        @block.scalar
        def _(act):
            nxt = Next(act)
            sq_at = [0]

            def evac(name, out, func=ACT.Copy, src=None, **kw):
                job_done(act, name)
                s, _ = bank_signal(name)
                act.activation(out, bank(name)[:, 0:out.shape[-1]] if src is None else src, func, **kw).then_inc(s, 1)

            def square(src):
                m = sq_at[0]
                sq_at[0] += 1
                if m >= 2:
                    act.wait_ge(*sq_release[m - 2])
                act.activation(SQ[:, m % 2, 0:src.shape[-1]], src, ACT.Square).then_inc(squared, 1)

            def root(name, width, n):
                evac(name, RS[:, rms_buffer[name], 0:width], ACT.Sqrt, bias=EPSC, scale=1.0 / n)

            def shift(n, out, off, lo, first):
                for t in range(KT):
                    nxt(scaled)
                    for a0, b0, m in parts_of(lo):
                        i = act.activation(out[:, t, a0 - off:b0 - off], out[:, t, a0 - off:b0 - off], ACT.Identity,
                                           bias=ADA[:, n, m, first + t:first + t + 1])
                    i.then_inc(h_set, 1)

            def modulation(n):
                for q in range(3):
                    evac(f"ada{n}.{q}", ADR[:, q, :])

            def block1():
                al = SP[:, 0, :]
                nxt(sp_abs)
                act.activation(SP[:, 1, :], al, ACT.Exp, scale=-1.0).then_inc(sp_exp, 1)
                nxt(sp_one)
                act.activation(SP[:, 3, :], SP[:, 2, :], ACT.Ln).then_inc(sp_ln, 1)
                act.wait_ge(x_in, 16)
                for t in range(KT):
                    square(X[:, t, S:TT])
                act.wait_ge(eps_set, 1)
                root("b1.pre", S, D)
                modulation(0)
                nxt(ada_set)
                shift(0, H1, S, S, 0)
                for t in range(KT):
                    evac(f"xr{t}", XR[:, t, 3:S + 3], ACT.Identity, bias=C("b_in", t))
                for t in range(KT):
                    evac(f"gr{t}", GG[:, t, :], ACT.Gelu_apprx_tanh, bias=C("b_in", 8 + t))
                act.wait_ge(q_bias_set, 1)
                for t in range(KT):
                    evac(f"q{t}", Q1[:, t, :], ACT.Identity, bias=QB[:, t:t + 1], scale=0.125)
                for g in range(4):
                    evac(f"k{g}", K1[:, g, :], ACT.Identity, bias=C("bk", g))
                for i in range(2):
                    evac(f"v{i}", V1[:, i, :])
                for part, buf, b0 in (("sr", SR, 28), ("sa", SA, 36)):
                    for t in range(KT):
                        evac(f"{part}{t}", buf[:, t, :], ACT.Sigmoid, bias=C("b_in", b0 + t))
                for part, buf, bias in (("ga", GA, "b_a"), ("gi", GI, "b_x")):
                    for t in range(KT):
                        evac(f"{part}{t}", buf[:, t, :], ACT.Sigmoid, bias=C(bias, t))
                nxt(sp_set)
                evacuated(act, "ga7")
                for t in range(KT):
                    act.activation(MU[:, t, :], GA[:, t, :], ACT.Tanh, scale=P8[:, t:t + 1]).then_inc(act_chain, 1)
                    act.wait_ge(act_chain, count(act_chain))
                    act.activation(GA[:, t, :], GA[:, t, :], ACT.Exp, scale=K8[:, t:t + 1]).then_inc(decay_set, 1)
                nxt(mult_sq)
                act.activation(V(22040, KT * S), V(22040, KT * S), ACT.Sqrt).then_inc(mult_set, 1)

                def probs(hd):
                    nxt(max_set)
                    st = ST1[:, hd % 2]
                    for b, (c0, c1) in enumerate(((0, 128), (128, 384))):
                        act.activation(P1[:, hd % 2, c0:c1], P1[:, hd % 2, c0:c1], ACT.Exp, bias=st[:, 1, b:b + 1],
                                       accum_out=st[:, 2, b:b + 1])
                    act.activation(st[:, 3, :], st[:, 1, :], ACT.Exp, bias=C("sinks", hd)).then_inc(prob_set, 1)

                probs(0)
                for hd in range(16):
                    if hd < 15:
                        probs(hd + 1)
                    p0 = 64 * (hd % 2)
                    evac(f"pt{hd}", PT1[:, hd % 2, :])
                    evac(f"o{hd}", Q1[p0:p0 + 64, hd // 2, :], src=bank(f"o{hd}")[p0:p0 + 64, 0:S])
                for t in range(KT):
                    evac(f"mx{t}", MX1[:, t, :])
                for t in range(KT):
                    evacuated(act, f"mx{t}")
                    square(MX1[:, t, :])
                root("b1.post", S, D)
                for t in range(KT):
                    nxt(x_set)
                    square(X[:, t, S:TT])
                root("b1.ffn", S, D)
                shift(0, H2, S, S, 24)

            def xe_evac():
                act.activation(XE, ps[2][:, :].rearrange("p (k m) -> p k m", k=KT), ACT.Copy).then_inc(xe_set, 1)

            def pgt_evac(par):
                act.activation(PGT[:, par, :], ps[3][:, 0:S], ACT.Copy).then_inc(pgt_set, 1)

            def gathers(gi, par):
                act.wait_ge(gathered, gi)
                xe_evac()
                act.wait_ge(gate_turned, gi)
                pgt_evac(par)

            def sigmoids(n):
                act.wait_ge(glu_set, n + 1)
                act.activation(SIG, GLU, ACT.Sigmoid, scale=ALPHA).then_inc(sig_set, 1)

            def rest(n, read):
                act.wait_ge(act_turned, n + 1)
                act.activation(AT, ps[4][:, :].rearrange("p (k m) -> p k m", k=4), ACT.Copy).then_inc(at_set, 1)
                act.wait_ge(moe_read, read)
                act.activation(YE, ps[5][:, :], ACT.Copy).then_inc(ye_set, 1)

            def moe():
                for i in range(2):
                    for half in range(2):
                        evac(f"ht{i}{half}", HT[:, i, 512 * half:512 * half + 512])
                for i in range(2):
                    nxt(rmax_set)
                    act.activation(EX[:, i, :], LG[:, i, 0:NE], ACT.Exp, bias=GST[:, i, 0:1]).then_inc(rexp_set, 1)
                modulation(1)
                job_done(act, "gt")
                s, _ = bank_signal("gt")
                act.activation(GATET[0:NE, :], bank("gt")[0:NE, 0:S], ACT.Copy).then_inc(s, 1)
                gathers(1, 0)
                with act.Fori(0, NE // 2) as it:
                    for u in range(2):
                        n = it * 2 + u
                        sigmoids(n)
                        gathers(n + 2, 1 - u)
                        rest(n, it * (2 * EC) + EC * (u + 1))
                act.wait_ge(lists_set, 1)
                n_over = act.value_load(lists[0:1, 2 * OVERMAX:2 * OVERMAX + 1], min_val=0, max_val=OVERMAX)
                with act.If(n_over > 0):
                    with act.Fori(0, n_over) as q:
                        gathers(q + (NE + 2), 0)
                        sigmoids(q + NE)
                        rest(q + NE, q * EC + EC * (NE + 1))
                with act.Else():
                    pass
                act.wait_ge(ff_done, 1)
                for t in range(KT):
                    square(FF[:, t, :])
                root("b1.out", S, D)

            def layer(l):
                lo = 0 if l == 0 else S
                s0 = lo // S
                act.wait_ge(x_in, 32)
                for t in range(KT):
                    nxt(x_set)
                    square(X[:, t, :])
                root(f"pre{l}", TT, D)
                shift(1 + l, H, 0, 0, 0)
                for c in range(2):
                    for t in (2 * c, 2 * c + 1):
                        evac(f"lg{l}.{t}", UC[:, t, lo:TT], ACT.Sigmoid)
                for part, buf, first in (("q", Q, lo), ("k", K, 0)):
                    for t in range(KT):
                        evac(f"{part}{l}.{t}", buf[:, t, first:TT])
                for c in range(4):
                    for i in (0, 2):
                        name = f"v{l}.{c}.{i}"
                        evac(name, VV[:, i:i + 2, 256 * c:256 * c + 256],
                             src=bank(name)[:, :].rearrange("p (i n) -> p i n", i=2))
                for t in range(4):
                    name = f"p{l}.{t}"
                    evac(name, PL[:, t, s0:2, 8:8 + S], src=segments(bank(name)[:, 0:TT - lo]))
                evac(f"lam{l}", LAME, ACT.Exp)
                groups = groups_of(l)

                def probs(gi):
                    hd, blocks, nk = groups[gi]
                    for j, b in enumerate(blocks):
                        for comp in range(2):
                            nxt(max_set)
                            st = ST[:, gi % 2, j, comp, :]
                            evac(f"s{l}.{gi}.{b}.{comp}", PR[:, gi % 2, j, comp, 0:nk], ACT.Exp,
                                 bias=st[:, 1:2], scale=0.125, accum_out=st[:, 2:3])

                nxt.n[id(max_set)] = 16 + 64 * l if "a" in phases else 64 * l
                probs(0)
                for gi, (hd, blocks, nk) in enumerate(groups):
                    if gi + 1 < len(groups):
                        probs(gi + 1)
                    for j, b in enumerate(blocks):
                        name = f"pt{l}.{gi}.{b}"
                        evac(name, AT2[:, gi % 2, 0:nk // 128, 128 * j:128 * j + 128],
                             src=bank(name)[:, 0:nk].rearrange("p (k q) -> p k q", q=128))
                    evac(f"o{l}.{gi}", Q[:, hd, blocks[0] * 128:blocks[0] * 128 + S])
                for hd in range(KT):
                    for gi, g in enumerate(groups):
                        if g[0] == hd:
                            evacuated(act, f"o{l}.{gi}")
                    square(Q[:, hd, lo:TT])
                    if hd:
                        if hd >= 3:
                            act.wait_ge(heads_normed, KT * l + hd - 2)
                        root(f"sub{l}.{hd - 1}", TT - lo, 128)
                act.wait_ge(heads_normed, KT * l + KT - 2)
                root(f"sub{l}.{KT - 1}", TT - lo, 128)
                for t in range(4):
                    nxt(centred)
                    square(UC[:, t, lo:TT])
                root(f"var{l}", TT - lo, 512)
                for t in range(4):
                    nxt(conv_scaled)
                    act.activation(UC[:, t, lo:TT], UC[:, t, lo:TT], ACT.Silu, bias=C(f"ln_b{l}", t),
                                   scale=C(f"ln_g{l}", t)).then_inc(conv_act, 1)
                for t in range(4):
                    evac(f"pm{l}.{t}", PO[:, t, lo:TT], ACT.Copy, scale=C(f"pool_scale{l}", t))
                ring_user = []
                for br in range(3):
                    for t in range(KT):
                        if len(ring_user) >= 4:
                            evacuated(act, ring_user[-4])
                        ring_user.append(f"y{l}.{br}.{t}")
                        evac(f"g{l}.{br}.{t}", GR[:, t % 4, lo:TT], ACT.Sigmoid, bias=C(f"b_gate{l}", 8 * br + t))
                for t in range(KT):
                    evac(f"m{l}.{t}", H[:, t, lo:TT])
                for t in range(KT):
                    evacuated(act, f"m{l}.{t}")
                    square(H[:, t, lo:TT])
                root(f"post{l}", TT - lo, D)
                if l == 0:
                    modulation(2)
                for t in range(KT):
                    nxt(x_set)
                    square(X[:, t, lo:TT])
                root(f"ffn{l}", TT - lo, D)
                shift(1 + l, H, 0, lo, 24)
                for t in range(FT):
                    evac(f"fg{l}.{t}", FA[:, t, lo:TT], ACT.Silu)
                for t in range(KT):
                    evac(f"f{l}.{t}", M[:, t, lo:TT])
                for t in range(KT):
                    evacuated(act, f"f{l}.{t}")
                    square(M[:, t, lo:TT])
                root(f"out{l}", TT - lo, D)

            act.wait_ge(consts_in, 32)
            act.activation(CSIG, C("c", 0, 24), ACT.Sigmoid).then_inc(silu_sig, 1)
            if "a" in phases:
                block1()
            if "b" in phases:
                moe()
            if "c" in phases:
                for l in range(LAYERS):
                    layer(l)

        @block.vector
        def _(dve):
            nxt = Next(dve)

            def link(ins, s=None):
                s = dve_chain if s is None else s
                ins.then_inc(s, 1)
                dve.wait_ge(s, count(s))

            def link_bank(ins, name):
                s, v = bank_signal(name)
                ins.then_inc(s, 1)
                dve.wait_ge(s, v)

            def stt(out, in0, scalar, in1, op0, op1, **kw):
                return dve.scalar_tensor_tensor(out=out, in0=in0, scalar=scalar, in1=in1, op0=op0, op1=op1, **kw)

            def modulation(n):
                for q in range(3):
                    name = f"adaT{n}.{q}"
                    job_done(dve, name)
                    src = bank(name)[:, :].rearrange("p (s j m) -> p j s m", s=4, j=4)
                    bias = C(f"b_ada{n}", 16 * q, 16).rearrange("p (j s) -> p j s", s=4)
                    ms = ((0, 0),) if n == 0 else ((0, 1), (1, 2))
                    for m, col in ms:
                        out = ADA[:, n, m, 16 * q:16 * q + 16].rearrange("p (j s) -> p j s", s=4)
                        i = dve.tensor_tensor(out, src[:, :, :, col], bias, ADD)
                        if m == ms[-1][0]:
                            link_bank(i, name)
                        else:
                            link(i)

            def pre_scale(n, gain, first):
                for m in range(1 if n == 0 else 2):
                    link(stt(CF[:, m, :], ADA[:, n, m, first:first + KT], 1.0, C(gain, 0, KT), ADD, MUL))

            def post_scale(n, gain, first):
                for m in range(1 if n == 0 else 2):
                    link(dve.tensor_tensor(CF[:, m, :], ADA[:, n, m, first:first + KT], C(gain, 0, KT), MUL))

            def inverse_rms(name, width):
                evacuated(dve, name)
                v = RS[:, rms_buffer[name], 0:width]
                link(dve.reciprocal(v, v))
                return v

            def pre_norm(name, out, off, lo):
                rs = inverse_rms(name, TT - lo)
                for t in range(KT):
                    for a0, b0, m in parts_of(lo):
                        i = stt(out[:, t, a0 - off:b0 - off], X[:, t, a0:b0], CF[:, m, t:t + 1],
                                rs[:, a0 - lo:b0 - lo], MUL, MUL)
                        if b0 == TT:
                            link(i, scaled)
                        else:
                            link(i)

            def post_norm(name, src, off, lo):
                rs = inverse_rms(name, TT - lo)
                for t in range(KT):
                    for a0, b0, m in parts_of(lo):
                        link(stt(tmp[:, a0 - lo:b0 - lo], src[:, t, a0 - off:b0 - off], CF[:, m, t:t + 1],
                                 rs[:, a0 - lo:b0 - lo], MUL, MUL))
                    link(dve.tensor_tensor(X[:, t, lo:TT], X[:, t, lo:TT], tmp[:, 0:TT - lo], ADD), x_set)

            def softplus():
                x = C("lam", 0, 8)
                al, e, w, ln, d, z, r, v, y, o = (SP[:, i, :] for i in range(10))
                link(stt(al, x, -1.0, x, MUL, MAX), sp_abs)
                nxt(sp_exp)
                link(dve.tensor_scalar(w, e, 1.0, None, ADD), sp_one)
                link(dve.tensor_scalar(d, w, -1.0, None, ADD))
                link(dve.tensor_scalar(z, d, 0.0, None, ALU.is_equal))
                link(dve.tensor_tensor(d, d, z, ADD))
                link(dve.reciprocal(r, d))
                nxt(sp_ln)
                link(dve.tensor_tensor(v, ln, e, MUL))
                link(dve.tensor_tensor(v, v, r, MUL))
                link(dve.tensor_tensor(y, z, e, MUL))
                link(dve.tensor_tensor(v, v, y, ADD))
                link(dve.tensor_scalar(o, x, -1.0, 0.0, MUL, MAX))
                link(dve.tensor_tensor(v, v, o, ADD))
                link(dve.tensor_scalar(K8, v, -8.0, None, MUL))
                link(dve.tensor_scalar(P8, v, 8.0, None, MUL), sp_set)

            def block1():
                softplus()
                link(dve.tensor_scalar(QB, C("b_in", 16, 8), 0.125, None, MUL), q_bias_set)
                link(dve.memset(XR[:, :, 0:3], 0.0))
                modulation(0)
                pre_scale(0, "pre_mix", 8)
                link(dve.tensor_copy(tmp[:, 0:1], ones[:, 0:1]), ada_set)
                pre_norm("b1.pre", H1, S, S)
                for t in range(KT):
                    evacuated(dve, f"xr{t}")
                    link(dve.tensor_scalar(XC[:, t, :], XR[:, t, 0:S], C("conv_w", t), C("conv_b", t), MUL, ADD))
                    for k in range(1, 4):
                        link(stt(XC[:, t, :], XR[:, t, k:k + S], C("conv_w", 8 * k + t), XC[:, t, :], MUL, ADD),
                             conv1_set if (t, k) == (KT - 1, 3) else None)
                dve.wait_ge(decay_set, KT)
                evacuated(dve, "gi7")
                n = KT * S
                den, mu, gi = V(2048, n), V(22040, n), V(10264, n)
                link(dve.tensor_scalar(den, mu, 1.0, None, ADD))
                link(dve.reciprocal(den, den))
                link(stt(mu, mu, 2.0, den, MUL, MUL), mult_sq)
                link(dve.tensor_tensor(gi, gi, V(4120, n), MUL))
                nxt(mult_set)
                link(dve.memset(MU[:, :, 0:1], 1.0))
                link(dve.tensor_tensor(gi, gi, mu, MUL))
                for t in range(KT):
                    link(dve.tensor_tensor_scan(XC[:, t, :], GA[:, t, :], GI[:, t, :], 0.0, MUL, ADD))
                link(dve.tensor_tensor(V(6168, n), V(6168, n), V(4120, n), MUL), rnn_set)
                dve.wait_ge(dist_in, 16)

                def maxima(hd):
                    job_done(dve, f"s{hd}")
                    if hd >= 2:
                        job_done(dve, f"pt{hd - 2}")
                    st = ST1[:, hd % 2]
                    link_bank(stt(P1[:, hd % 2, :], DIST, -slopes[hd], bank(f"s{hd}")[:, 0:NDIST], MUL, ADD), f"s{hd}")
                    link(dve.reduce_max(st[:, 0, 0:1], P1[:, hd % 2, 0:128], axis=AX.X))
                    link(dve.reduce_max(st[:, 0, 1:2], P1[:, hd % 2, 128:384], axis=AX.X))
                    link(dve.tensor_scalar(st[:, 1, :], st[:, 0, :], C("sinks", hd), -1.0, MAX, MUL), max_set)

                maxima(0)
                for hd in range(16):
                    if hd < 15:
                        maxima(hd + 1)
                    st = ST1[:, hd % 2]
                    nxt(prob_set)
                    link(dve.tensor_tensor(st[:, 2, :], st[:, 2, :], st[:, 3, :], ADD))
                    link(dve.reciprocal(st[:, 2, :], st[:, 2, :]))
                    link(dve.tensor_scalar(P1[:, hd % 2, 0:128], P1[:, hd % 2, 0:128], st[:, 2, 0:1], None, MUL))
                    link(dve.tensor_scalar(P1[:, hd % 2, 128:384], P1[:, hd % 2, 128:384], st[:, 2, 1:2], None, MUL),
                         prob_normed)
                evacuated(dve, "sa7")
                for c in range(4):
                    for t in (2 * c, 2 * c + 1):
                        job_done(dve, f"yr{t}")
                        link_bank(dve.tensor_tensor(M1[:, t, :], bank(f"yr{t}")[:, 0:S], SR[:, t, :], MUL), f"yr{t}")
                    for t in (2 * c, 2 * c + 1):
                        job_done(dve, f"ya{t}")
                        link_bank(dve.tensor_tensor(tmp[:, 0:S], bank(f"ya{t}")[:, 0:S], SA[:, t, :], MUL), f"ya{t}")
                        link(dve.tensor_tensor(M1[:, t, :], M1[:, t, :], tmp[:, 0:S], ADD), merged)
                post_scale(0, "post_mix", 16)
                post_norm("b1.post", MX1, S, S)
                pre_scale(0, "pre_ffn", 32)
                pre_norm("b1.ffn", H2, S, S)

            def select(e, slots, bpar):
                for i in range(2):
                    dve.tensor_scalar(PSEL[:, i, :], slots, POS[:, i, bass.ds(e, 1)], None, ALU.is_equal)
                    dve.tensor_scalar(GSEL[:, i, :], slots, POS[:, i, bass.ds(e, 1)],
                                      GATE[:, i, bass.ds(e, 1)], ALU.is_equal, MUL)
                dve.tensor_scalar(BSEL[:, bpar, :], ones[:, 0:SLOT], ident[:, bass.ds(e, 1)], None, MUL)\
                    .then_inc(sel_set, 1)

            def swiglu(n, read):
                dve.wait_ge(moe_read, read)
                h = [ps[b][:, :].rearrange("p (f two) -> p f two", two=2) for b in range(2)]
                for b in range(2):
                    i = dve.tensor_scalar(GLU[:, 256 * b:256 * b + 256], h[b][:, :, 0], LIMIT, None, MIN)
                i.then_inc(glu_set, 1)
                for b in range(2):
                    i = dve.tensor_scalar(LIN[:, 256 * b:256 * b + 256], h[b][:, :, 1], LIMIT, -LIMIT, MIN, MAX)
                i.then_inc(lin_set, 1)
                dve.wait_ge(lin_set, n + 1)
                dve.wait_ge(sig_set, n + 1)
                dve.tensor_tensor(AC, GLU, SIG, MUL).then_inc(half_act, 1)
                dve.wait_ge(half_act, n + 1)
                stt(AC, LIN, 1.0, AC, ADD, MUL).then_inc(act_set, 1)

            def add_rows(n, sc):
                for r in range(2):
                    dve.wait_ge(scattered, sc + r)
                    for half in range(2):
                        f0 = 4 * half + 2 * r
                        v = work[:, 4096 + f0 * S:4096 + (f0 + 2) * S]
                        i = dve.tensor_tensor(v, v, ps[(0, 6)[r] + half][:, :], ADD)
                    i.then_inc((added0, added1)[r], 1)
                dve.wait_ge(added1, n + 1)

            def moe():
                dve.wait_ge(moe_consts_in, 16 * 4)
                link(dve.memset(LG[:, :, NE:NE + 8], -BIG))
                link(dve.memset(M8[:, :, 12:16], -BIG))
                link(dve.memset(GATE[:, :, NE:NE + 2], 0.0))
                link(dve.memset(POS[:, :, NE:NE + 2], -1.0))
                for i in range(2):
                    job_done(dve, f"lg{i}")
                    link_bank(dve.tensor_copy(LG[:, i, 0:NE], bank(f"lg{i}")[:, 0:NE]), f"lg{i}")
                    link(dve.max(M8[:, i, 0:8], LG[:, i, 0:NE]))
                    link(dve.tensor_scalar(GST[:, i, 0:1], M8[:, i, 0:1], -1.0, None, MUL), rmax_set)
                    link(dve.tensor_copy(M8[:, i, 8:12], M8[:, i, 0:4]))
                    link(dve.match_replace(LR[:, i, :], M8[:, i, 8:16], LG[:, i, :], BIG))
                    link(dve.tensor_tensor(MK[:, i, :], LR[:, i, 0:NE], LG[:, i, 0:NE], ALU.not_equal), mask_set)
                for i in range(2):
                    nxt(rexp_set)
                    link(dve.tensor_tensor(EX[:, i, :], EX[:, i, :], MK[:, i, :], MUL))
                    link(dve.reduce_sum(GST[:, i, 1:2], EX[:, i, :], axis=AX.X))
                    link(dve.reciprocal(GST[:, i, 2:3], GST[:, i, 1:2]))
                    link(dve.tensor_scalar(GATE[:, i, 0:NE], EX[:, i, :], GST[:, i, 2:3], None, MUL), gate_set)
                modulation(1)
                for i in range(2):
                    job_done(dve, f"pos{i}")
                    link_bank(stt(POS[:, i, 0:NE], bank(f"pos{i}")[:, 0:NE], 1.0, MK[:, i, :], ADD, MUL), f"pos{i}")
                    link(dve.tensor_scalar(POS[:, i, 0:NE], POS[:, i, 0:NE], -1.0, None, ADD))
                job_done(dve, "cnt")
                for r in range(3):
                    i = dve.tensor_scalar(OFLAG[0:1, r * NE:(r + 1) * NE], bank("cnt")[0:1, 0:NE],
                                          float(SLOT * (r + 1)), None, ALU.is_gt)
                    if r < 2:
                        link(i)
                    else:
                        link_bank(i, "cnt")
                link(dve.tensor_tensor_scan(OCUM[0:1, :], ones[0:1, 0:OVER], OFLAG[0:1, :], 0.0, MUL, ADD))
                link(dve.tensor_tensor(OEXP[0:1, :], OFLAG[0:1, :], route_table("expert_of")[0:1, :], MUL))
                link(dve.tensor_tensor(ORND[0:1, :], OFLAG[0:1, :], route_table("round_of")[0:1, :], MUL))
                for s in range(OVERMAX):
                    for at, src in ((0, OEXP), (OVERMAX, ORND)):
                        link(stt(OJUNK[0:1, :], OCUM[0:1, :], float(s + 1), src[0:1, :], ALU.is_equal, MUL,
                                 accum_out=OLIST[0:1, at + s:at + s + 1]))
                link(dve.tensor_copy(lists[0:1, 0:2 * OVERMAX], OLIST[0:1, :]))
                link(dve.tensor_copy(lists[0:1, 2 * OVERMAX:2 * OVERMAX + 1], OCUM[0:1, OVER - 1:OVER]), lists_set)
                for j in range(4):
                    job_done(dve, f"b2{j}")
                    link_bank(dve.tensor_copy(work[:, 4096 + 2 * j * S:4096 + 2 * (j + 1) * S], bank(f"b2{j}")[:, :]),
                              f"b2{j}")
                first = route_table("slots")[:, 0:128]
                select(0, first, 0)
                dve.wait_ge(gathered, 1)
                dve.wait_ge(gate_turned, 1)
                select(1, first, 1)
                with dve.Fori(0, NE // 2) as it:
                    for u in range(2):
                        n = it * 2 + u
                        swiglu(n, it * (2 * EC) + EC * u + KT)
                        dve.wait_ge(gathered, n + 2)
                        dve.wait_ge(gate_turned, n + 2)
                        select(n + 2, first, u)
                        add_rows(n, it * 4 + 2 * u + 1)
                n_over = dve.value_load(lists[0:1, 2 * OVERMAX:2 * OVERMAX + 1], min_val=0, max_val=OVERMAX)
                dve.wait_ge(sel_set, NE + 2)
                with dve.If(n_over > 0):
                    with dve.Fori(0, n_over) as q:
                        e = dve.value_load(lists[0:1, bass.ds(q, 1)], min_val=0, max_val=NE - 1)
                        r = dve.value_load(lists[0:1, bass.ds(q + OVERMAX, 1)], min_val=0, max_val=3)
                        select(e, route_table_at("slots", r), 0)
                        swiglu(q + NE, q * EC + (EC * NE + KT))
                        add_rows(q + NE, q * 2 + (2 * NE + 1))
                with dve.Else():
                    pass
                link(dve.tensor_copy(tmp[:, 0:1], ones[:, 0:1]), ff_done)
                post_scale(0, "post_ffn", 40)
                post_norm("b1.out", FF, S, S)

            def route_table_at(name, r):
                return work[:, bass.ds(r * 128 + 15448, 128)]

            def layer(l):
                lo = 0 if l == 0 else S
                s0 = lo // S
                n = 1 + l
                width = TT - lo
                pre_scale(n, f"pre_mix{l}", 8)
                pre_norm(f"pre{l}", H, 0, 0)
                link(dve.tensor_tensor(LAMP, C(f"lam_qk{l}", 0, 4).rearrange("p (n two) -> p n two", two=2)[:, :, 0],
                                       C(f"lam_qk{l}", 0, 4).rearrange("p (n two) -> p n two", two=2)[:, :, 1], MUL),
                     lam_prod)
                link(dve.tensor_scalar(SUBG, C(f"subln{l}"), 1.0 - lam_init[l], None, MUL))
                link(dve.memset(U[:, :, :, 0:TAPS // 2], 0.0))
                link(dve.memset(U[:, :, :, S + TAPS // 2:S + TAPS - 1], 0.0))
                for t in range(4):
                    evacuated(dve, f"lg{l}.{t}")
                    name = f"la{l}.{t}"
                    job_done(dve, name)
                    link_bank(dve.tensor_tensor(U[:, t, s0:2, TAPS // 2:TAPS // 2 + S],
                                                segments(bank(name)[:, 0:width]), segments(UC[:, t, lo:TT]), MUL), name)
                for k in range(TAPS):
                    for t in range(4):
                        src = U[:, t, s0:2, k:k + S]
                        out = segments(UC[:, t, lo:TT])
                        if k == 0:
                            link(dve.tensor_scalar(out, src, C(f"taps{l}", t), C(f"tap_b{l}", t), MUL, ADD))
                        else:
                            link(stt(out, src, C(f"taps{l}", 4 * k + t), out, MUL, ADD))
                for t in range(KT):
                    for part, view in (("q", Q), ("k", K)):
                        name = f"rot{part}{l}.{t}"
                        job_done(dve, name)
                        link_bank(dve.tensor_tensor(tmp[:, 0:S], bank(name)[:, 0:S], sin, MUL), name)
                        link(dve.tensor_tensor(view[:, t, S:TT], view[:, t, S:TT], cos, MUL))
                        link(dve.tensor_tensor(view[:, t, S:TT], view[:, t, S:TT], tmp[:, 0:S], ADD),
                             rotated if (t, part) == (KT - 1, "k") else None)
                evacuated(dve, f"lam{l}")
                link(dve.tensor_scalar(NLAM, LAME[:, 1:2], lam_init[l], LAME[:, 0:1], SUB, SUB))
                groups = groups_of(l)

                def maxima(gi):
                    hd, blocks, nk = groups[gi]
                    for j, b in enumerate(blocks):
                        for comp in range(2):
                            name = f"s{l}.{gi}.{b}.{comp}"
                            job_done(dve, name)
                            st = ST[:, gi % 2, j, comp, :]
                            link(dve.reduce_max(st[:, 0:1], bank(name)[:, 0:nk], axis=AX.X))
                            link(dve.tensor_scalar(st[:, 1:2], st[:, 0:1], -0.125, None, MUL), max_set)

                maxima(0)
                for gi, (hd, blocks, nk) in enumerate(groups):
                    if gi + 1 < len(groups):
                        maxima(gi + 1)
                    for j, b in enumerate(blocks):
                        p = [PR[:, gi % 2, j, comp, 0:nk] for comp in range(2)]
                        st = [ST[:, gi % 2, j, comp, :] for comp in range(2)]
                        evacuated(dve, f"s{l}.{gi}.{b}.0")
                        evacuated(dve, f"s{l}.{gi}.{b}.1")
                        link(dve.reciprocal(st[0][:, 3:4], st[0][:, 2:3]))
                        link(dve.reciprocal(st[1][:, 3:4], st[1][:, 2:3]))
                        link(dve.tensor_tensor(st[1][:, 4:5], st[1][:, 3:4], NLAM, MUL))
                        link(dve.tensor_scalar(p[0], p[0], st[0][:, 3:4], None, MUL))
                        link(stt(p[0], p[1], st[1][:, 4:5], p[0], MUL, ADD), prob_normed)
                for hd in range(KT):
                    rs = inverse_rms(f"sub{l}.{hd}", width)
                    link(stt(Q[:, hd, lo:TT], Q[:, hd, lo:TT], SUBG, rs[:, 0:width], MUL, MUL), heads_normed)
                name = f"mean{l}"
                job_done(dve, name)
                link_bank(dve.tensor_scalar(tmp[:, 0:width], bank(name)[:, 0:width], 1.0 / 512, None, MUL), name)
                for t in range(4):
                    link(dve.tensor_tensor(UC[:, t, lo:TT], UC[:, t, lo:TT], tmp[:, 0:width], SUB), centred)
                rs = inverse_rms(f"var{l}", width)
                for t in range(4):
                    link(dve.tensor_tensor(UC[:, t, lo:TT], UC[:, t, lo:TT], rs[:, 0:width], MUL), conv_scaled)
                for br in range(3):
                    for t in range(KT):
                        name = f"y{l}.{br}.{t}"
                        evacuated(dve, f"g{l}.{br}.{t}")
                        job_done(dve, name)
                        if br == 0:
                            link_bank(dve.tensor_tensor(M[:, t, lo:TT], bank(name)[:, 0:width], GR[:, t % 4, lo:TT],
                                                        MUL), name)
                        else:
                            link_bank(dve.tensor_tensor(tmp[:, 0:width], bank(name)[:, 0:width],
                                                        GR[:, t % 4, lo:TT], MUL), name)
                            link(dve.tensor_tensor(M[:, t, lo:TT], M[:, t, lo:TT], tmp[:, 0:width], ADD),
                                 merged if br == 2 else None)
                post_scale(n, f"post_mix{l}", 16)
                post_norm(f"post{l}", H, 0, lo)
                if l == 0:
                    modulation(2)
                pre_scale(n, f"pre_ffn{l}", 32)
                pre_norm(f"ffn{l}", H, 0, lo)
                for t in range(FT):
                    name = f"fu{l}.{t}"
                    evacuated(dve, f"fg{l}.{t}")
                    job_done(dve, name)
                    link_bank(dve.tensor_tensor(FA[:, t, lo:TT], FA[:, t, lo:TT], bank(name)[:, 0:width], MUL), name)
                post_scale(n, f"post_ffn{l}", 40)
                post_norm(f"out{l}", M, 0, lo)

            link(dve.memset(EPSC, EPS), eps_set)
            link(dve.memset(cstat[:, :], 0.0))
            dve.wait_ge(silu_sig, 1)
            link(dve.tensor_tensor(CS[:, :, 0:3].rearrange("p k m -> p m k"), C("c", 0, 24).rearrange("p (m k) -> p m k", m=3),
                                   CSIG.rearrange("p (m k) -> p m k", m=3), MUL), silu_set)
            if "a" in phases:
                block1()
            if "b" in phases:
                moe()
            if "c" in phases:
                for l in range(LAYERS):
                    layer(l)


def column_array(inputs):
    out = np.zeros((128, NCOL), np.float32)

    def put(name, v, at=0):
        v = np.asarray(v).reshape(-1, 128).T
        c = COLS[name][0] + at
        out[:, c:c + v.shape[1]] = v

    put("c", inputs["c"])
    put("c", inputs["c_2"], 8)
    put("c", inputs["c_ctx_2"], 16)
    put("b_ada0", inputs["b_ada"])
    put("b_ada1", inputs["b_mod_2"][0])
    put("b_ada2", inputs["b_mod_2"][1])
    for name, src in (("pre_mix", "norm_pre_mix"), ("post_mix", "norm_post_mix"), ("pre_ffn", "norm_pre_ffn"),
                      ("post_ffn", "norm_post_ffn"), ("b_in", "b_in"), ("conv_w", "conv_w"), ("conv_b", "conv_b"),
                      ("b_a", "rg_b_a"), ("b_x", "rg_b_x"), ("lam", "rg_lambda")):
        put(name, inputs[src])
    bk = np.asarray(inputs["b_in"])[0, 3072:3328].reshape(4, 64)
    put("bk", np.concatenate([bk, bk], axis=1))
    c = COLS["sinks"][0]
    out[:, c:c + 16] = np.asarray(inputs["attn_sinks"])
    for l in range(LAYERS):
        for name, src in (("pre_mix", "g_pre_mix_2"), ("post_mix", "g_post_mix_2"), ("pre_ffn", "g_pre_ffn_2"),
                          ("post_ffn", "g_post_ffn_2"), ("b_gate", "b_gate_2"), ("taps", "conv_w_2"),
                          ("tap_b", "conv_b_2"), ("ln_g", "conv_ln_g_2"), ("ln_b", "conv_ln_b_2"),
                          ("subln", "subln_g_2"), ("pool_scale", "pool_scale_2")):
            put(f"{name}{l}", inputs[src][l])
        c = COLS[f"lam_qk{l}"][0]
        for i, src in enumerate(("lam_q1_2", "lam_k1_2", "lam_q2_2", "lam_k2_2")):
            out[0:64, c + i] = np.asarray(inputs[src][l])
    return out


def kept_tables():
    out = np.zeros((128, NKEPT), np.float32)
    out[:, 0:128] = np.eye(128)
    f = np.arange(128)
    low = f % 32 < 16
    out[f[low] + 16, 128 + f[low]] = -1.0
    out[f[~low] - 16, 128 + f[~low]] = 1.0
    t = np.arange(S)
    inv = (10000.0 ** (-np.arange(0, 32, 2, dtype=np.float32) / 32)).astype(np.float32)
    place = np.where((f % 64 < 32)[:, None], (t // 64)[None], (t % 64)[None]).astype(np.float32)
    angle = place * inv[f % 16][:, None]
    out[:, 256:512] = np.cos(angle)
    out[:, 512:768] = np.sin(angle)
    for g in range(4):
        w = 2 << g
        t = np.concatenate([np.arange(8), np.arange(S - 8, S)])
        n = np.minimum(t + w // 2, S) - np.maximum(t - w // 2, 0)
        out[:, 768 + 16 * g:784 + 16 * g] = w / n
    return out


def route_tables():
    out = np.zeros((128, NROUTE), np.float32)
    out[:, 0:512] = np.concatenate([SLOT * r + np.arange(128) % SLOT for r in range(4)])
    out[:, 512:640] = np.triu(np.ones((128, 128)), 1)
    out[:, 640:640 + OVER] = np.arange(OVER) % NE
    out[:, 640 + OVER:] = np.arange(OVER) // NE + 1
    return out


def distances():
    q, c = np.arange(128)[:, None], np.arange(128)[None]
    near = q - c
    dist = np.concatenate([near, near + 128, near], axis=1).astype(np.float32)
    return np.where((dist >= 0) & (dist < 128), dist, np.float32(FAR)).astype(np.float32)


def laid_out(inputs):
    arrays = {"cols": column_array(inputs), "kept": kept_tables(), "route": route_tables(), "dist": distances()}
    arrays["rows"] = np.concatenate([np.asarray(inputs["b_in"])[0, 3328:3584],
                                     np.asarray(inputs["router_b"])[0]])[None]
    arrays["x"] = np.ascontiguousarray(np.asarray(inputs["x"])[0].T)
    arrays["ctx"] = np.ascontiguousarray(np.asarray(inputs["ctx_2"])[0].T)
    for name in ("w_ada", "w_in", "rg_w_a", "rg_w_x", "w_o_rnn", "w_o_attn", "w_out", "router_w",
                 "moe_w1", "moe_w2", "moe_b1", "moe_b2"):
        arrays[name] = np.asarray(inputs[name])[0]
    for name in ("w_mod_2", "w_in_2", "w_conv_out_2", "w_attn_out_2", "w_pool_group_2", "w_pool_out_2",
                 "w_out_2", "w_ffn_in_2", "w_ffn_out_2"):
        arrays[name] = np.asarray(inputs[name])
    return arrays


def kernel(**inputs):
    import concourse.bacc as bacc
    from concourse.bass_utils import run_bass_kernel_spmd

    nc = bacc.Bacc("TRN2", target_bir_lowering=False, num_devices=1)
    arrays = laid_out(inputs)
    aps = {name: nc.dram_tensor(f"in_{name}", v.shape, mybir.dt.from_np(v.dtype), kind="ExternalInput").ap()
           for name, v in arrays.items()}
    aps["out"] = nc.dram_tensor("out_t", (D, S), mybir.dt.float32, kind="ExternalOutput").ap()
    build_program(nc, aps)
    r = run_bass_kernel_spmd(nc, [{f"in_{name}": v for name, v in arrays.items()}], core_ids=[0])
    return np.ascontiguousarray(r.results[0]["out_t"].T)[None]
```

```python
import math
from contextlib import ExitStack

import numpy as np
import concourse.bass as bass
from concourse import mybir

D = 1024
KT = D // 128
S = 256
TT = 2 * S
NE = 32
DFF = 2816
FT = DFF // 128
TAPS = 31
EPS = 1e-6
LIMIT = 7.0
ALPHA = 1.702
SLOT = 64
NSLOT = 8
SLOTW = 2048
NSLOT2 = 3
NSPLIT = 3
FRONT = 4096
BANKS = 7
MODBANK = 7
OVERMAX = 16
OVER = 3 * NE
EC = 12
OSLOT = 6
BIG = 3.0e38
FAR = 1.0e30
LAYERS = 2
HALF = FT // 2


def packed_columns():
    names = [("c", 24), ("b_ada0", 48), ("b_ada1", 48), ("b_ada2", 48),
             ("pre_mix", 8), ("post_mix", 8), ("pre_ffn", 8), ("post_ffn", 8), ("b_in", 44), ("bk", 4),
             ("conv_w", 32), ("conv_b", 8), ("b_a", 8), ("b_x", 8), ("lam", 8), ("sinks", 16)]
    for l in range(LAYERS):
        names += [(f"pre_mix{l}", 8), (f"post_mix{l}", 8), (f"pre_ffn{l}", 8), (f"post_ffn{l}", 8),
                  (f"b_gate{l}", 24), (f"taps{l}", 4 * TAPS), (f"tap_b{l}", 4), (f"ln_g{l}", 4),
                  (f"ln_b{l}", 4), (f"subln{l}", 1), (f"pool_scale{l}", 4), (f"lam_qk{l}", 4)]
    at, out = 0, {}
    for name, k in names:
        out[name] = (at, k)
        at += k
    return out, at


def modulation_steps(parts):
    out, ready = [], None
    for n, q in parts:
        for k in range(KT):
            out.append([("mod", n, q, k)])
            if k == 0 and ready:
                out[-1].append(("modT",) + ready)
        ready = (n, q)
    out.append([("modT",) + ready])
    return out


def spread(jobs, slots):
    out, at = [], 0
    for i, job in enumerate(jobs):
        out.append(job)
        n = (i + 1) * len(slots) // len(jobs)
        for slot in slots[at:n]:
            out += slot
        at = n
    return out


def slots_of(n):
    out = []
    for k in range(n + 2):
        slot = []
        if 1 <= k <= n:
            slot.append(("T", k - 1))
        if k >= 2:
            slot.append(("O", k - 2))
        if k < n:
            slot.append(("S", k))
            if k + 1 < n:
                slot.append(("Z", k + 1))
        out.append(slot)
    return out


def filled(steps, fill, after):
    out = []
    for step in steps:
        out.append(step)
        if fill and after(step):
            out += fill.pop(0)
    return out


def block1_steps():
    def lin(part, n):
        return [("lin", part, t) for t in range(n)]

    fill = modulation_steps([(0, 1), (0, 2), (1, 0), (1, 1), (1, 2)])
    first = lin("xr", 8) + lin("gr", 8) + lin("q", 8)
    first += [("gates",)] + [("k",), ("v",), ("mult",), ("Z", 0)]
    steps = filled(first, fill, lambda s: s[0] in "kv" or s[0] == "lin" and s[2] % 2)
    steps += filled(spread(lin("sr", 8) + lin("sa", 8), slots_of(16)), fill, lambda s: s[0] == "S")
    last = []
    for c in range(4):
        for part in ("yr", "ya"):
            last += [("lin", part, 2 * c), ("lin", part, 2 * c + 1)]
    steps += filled(last, fill, lambda s: True)
    assert not fill
    return steps


def groups_of(l):
    return [g for hd in range(8) for g in (([(hd, (0, 1), S)] if l == 0 else []) + [(hd, (2, 3), TT)])]


def layer_steps(l):
    def lin(part, ts):
        return [("lin", part, t) for t in ts]

    steps = []
    for c in range(2):
        steps += lin("lg", (2 * c, 2 * c + 1)) + lin("la", (2 * c, 2 * c + 1))
    n = len(groups_of(l))
    slots = slots_of(n)
    at = 0
    for c in range(4):
        jobs = lin("q", (2 * c, 2 * c + 1)) + lin("k", (2 * c, 2 * c + 1)) + [("v", c, 0), ("v", c, 2)]
        if c == 0:
            steps += jobs
        else:
            steps += spread(jobs, slots[at:at + n // 4])
            at += n // 4
        steps.append(("rot", c))
        if c == 0:
            steps.append(("Z", 0))
    steps += spread(lin("p", range(4)), slots[at:])
    taps = [("conv", t, part) for t in range(4) for part in range(4)]
    taps = [taps[2 * i:2 * i + 2] for i in range(4)] + [[s] for s in taps[8:]]
    steps = filled(steps, taps, lambda s: s[0] == "lin" and s[1] not in ("lg", "la") or s[1:] in (("lg", 2), ("lg", 3), ("la", 2), ("la", 3)))
    assert not taps
    tail = [("mean",), ("gate", 0, 0), ("var",), ("gate", 0, 1), ("square", 0), ("conv_root",)]
    pending = []
    for hd in range(KT):
        pending.append([("sub", hd)] + ([("square", hd + 1)] if hd < KT - 1 else [])
                       + ([("sub_root", hd - 1)] if hd else []))
    pending.append([("sub_root", KT - 1)])
    tail += [("gate", 0, 2)] + pending.pop(0) + [("gate", 0, 3)] + pending.pop(0)
    ys = [("y", 0, t) for t in range(4)] + [("gate", 0, t) for t in range(4, 8)] + [("y", 0, t) for t in range(4, 8)]
    for step in ys:
        tail.append(step)
        if pending:
            tail += pending.pop(0)
    for t in range(0, KT, 2):
        tail += [("gate", 1, t), ("gate", 1, t + 1), ("pool", t // 2), ("y", 1, t), ("y", 1, t + 1)]
    tail.append(("mix",))
    for t in range(0, KT, 4):
        tail += [("gate", 2, t + i) for i in range(4)] + [("y", 2, t + i) for i in range(4)]
    steps += tail
    if l == 0:
        fill = modulation_steps([(2, 0), (2, 1), (2, 2)])
        steps = filled(steps, fill, lambda s: s[0] == "S" or s[0] == "lin" and s[1] in ("lg", "la", "p"))
        assert not fill
    return steps


COLS, NCOL = packed_columns()
KEPT = {"ident": (0, 128), "rot": (128, 128), "cos": (256, S), "sin": (512, S), "edge": (768, 64)}
NKEPT = 832
ROUTE = {"slots": (0, 1024), "before": (1024, 128), "expert_of": (1152, OVER), "round_of": (1152 + OVER, OVER)}
NROUTE = 1152 + 2 * OVER
NDIST = 384


def build_program(nc, a, phases="abc"):
    f32, f32r, i32 = mybir.dt.float32, mybir.dt.float32r, mybir.dt.int32
    ALU, ACT, AX = mybir.AluOpType, mybir.ActivationFunctionType, mybir.AxisListType
    ADD, SUB, MUL, MAX, MIN = ALU.add, ALU.subtract, ALU.mult, ALU.max, ALU.min
    slopes = [2.0 ** (-8.0 * (h + 1) / 16) for h in range(16)]
    lam_init = [0.8 - 0.6 * math.exp(-0.3 * l) for l in range(LAYERS)]

    ctx = ExitStack()
    with ctx:
        def sb(name, width, dt=f32):
            return ctx.enter_context(nc.sbuf_tensor(name, [128, width], dt))

        def sem(name):
            return ctx.enter_context(nc.semaphore(name))

        cols = sb("cols", NCOL)
        kept = sb("kept", NKEPT)
        ones = sb("ones", 128)
        ada = sb("ada", 3 * 96)
        resid = sb("resid", KT * TT)
        work = sb("work", 4 * 4096 + 6512)
        sq = sb("sq", 2 * TT)
        rs = sb("rs", 2 * TT)
        tmp = sb("tmp", TT)
        coef = sb("coef", 2 * KT)
        small = sb("small", 272)
        lists = sb("lists", 2 * OVERMAX + 1, i32)
        cstat = sb("cstat", KT * 32)
        poolw = sb("poolw", 512)
        with ExitStack() as early:
            front = early.enter_context(nc.sbuf_tensor("front", [128, FRONT], f32))
            ring = early.enter_context(nc.sbuf_tensor("ring", [128, NSLOT * SLOTW], f32))
        h_hi = sb("h_hi", KT * TT, f32r)
        ring2 = sb("ring2", NSLOT2 * SLOTW)
        wsplit = sb("wsplit", NSPLIT * 2 * D, f32r)
        h_lo = sb("h_lo", KT * TT, f32r)
        ps = [ctx.enter_context(nc.psum_tensor(f"bank{i}", [128, 512], f32)) for i in range(BANKS + 1)]

        def V(base, *dims):
            n = math.prod(dims)
            v = front[:, base:base + n] if base < FRONT else work[:, base - FRONT:base - FRONT + n]
            if len(dims) == 2:
                return v.rearrange("p (a b) -> p a b", a=dims[0])
            if len(dims) == 3:
                return v.rearrange("p (a b c) -> p a b c", a=dims[0], b=dims[1])
            if len(dims) == 4:
                return v.rearrange("p (a b c d) -> p a b c d", a=dims[0], b=dims[1], c=dims[2])
            return v

        def C(name, i=0, n=1):
            return cols[:, COLS[name][0] + i:COLS[name][0] + i + n]

        def kept_table(name):
            at, w = KEPT[name]
            return kept[:, at:at + w]

        X = resid[:, :].rearrange("p (k t) -> p k t", k=KT)
        CS = cstat[:, :].rearrange("p (k m) -> p k m", k=KT)
        SQ = sq[:, :].rearrange("p (b t) -> p b t", b=2)
        ADA = ada[:, :].rearrange("p (n m f) -> p n m f", n=3, m=2)
        CF = coef[:, :].rearrange("p (m k) -> p m k", m=2)
        ADR = poolw[:, :]
        POOLW = poolw[:, :].rearrange("p (g d) -> p g d", g=4)
        CSIG = small[:, 0:24]
        SP = small[:, 24:104].rearrange("p (n k) -> p n k", n=10)
        K8, P4 = small[:, 104:112], small[:, 112:120]
        LAMP, LAME, NLAM, SUBG = small[:, 120:122], small[:, 122:124], small[:, 124:125], small[:, 125:126]
        EPSC = small[:, 134:135]
        RS = rs[:, :].rearrange("p (b t) -> p b t", b=2)
        QB = small[:, 126:134]
        ST1 = small[:, 136:152].rearrange("p (b n k) -> p b n k", b=2, n=4)
        ST = small[:, 152:216].rearrange("p (g b c n) -> p g b c n", g=2, b=2, c=2)
        GST = small[:, 216:232].rearrange("p (i n) -> p i n", i=2)
        ident, rot = kept_table("ident"), kept_table("rot")
        cos, sin = kept_table("cos"), kept_table("sin")
        edge = kept_table("edge").rearrange("p (g e) -> p g e", g=4)

        H1 = V(0, KT, S)
        XR = V(4096, KT, S + 3)
        XC = V(6168, KT, S)
        GG = V(2048, KT, S)
        GA = V(8216, KT, S)
        GI = V(10264, KT, S)
        Q1 = V(12312, KT, S)
        K1 = V(14360, 4, S)
        V1 = V(15384, 2, S)
        SR = V(15896, KT, S)
        SA = V(17944, KT, S)
        BD = V(19992, 2, KT, 128)
        MU = V(22040, KT, S)
        P1 = V(24088, 2, NDIST)
        PT1 = V(24856, 2, NDIST)
        DIST = V(25624, NDIST)
        ROWS = V(26008, S + NE)
        M1 = V(4096, KT, S)
        MX1 = H1
        H2 = V(0, KT, S)
        HT = V(2048, 2, D)
        FF = V(4096, KT, S)
        B1 = V(6144, 2 * D)
        at = [8192]

        def moe_view(*dims):
            at[0] += math.prod(dims)
            return V(at[0] - math.prod(dims), *dims)

        XE = moe_view(KT, SLOT)
        PSEL = moe_view(2, SLOT)
        GSEL = moe_view(2, 2, 128)
        PGT = moe_view(2, 2, S)
        GLU, SIG, LIN, AC = (moe_view(512) for _ in range(4))
        AT = moe_view(4, 128)
        YE = moe_view(512)
        B2 = moe_view(D)
        RW = moe_view(KT, NE)
        LG, LR = moe_view(2, NE + 8), moe_view(2, NE + 8)
        MK = moe_view(2, NE)
        GATE = moe_view(2, NE + 2)
        POS = moe_view(2, NE + 2)
        EX = moe_view(2, NE)
        BSEL = moe_view(2, SLOT)
        GATET = moe_view(S)
        M8 = moe_view(2, 16)
        OFLAG, OCUM, OEXP, ORND, OJUNK = (moe_view(OVER) for _ in range(5))
        OLIST = moe_view(2 * OVERMAX)
        rt_at = at[0]
        RT = moe_view(NROUTE)

        def route_table(name):
            at, w = ROUTE[name]
            return RT[:, at:at + w]

        before = route_table("before")
        HH, HL = (t[:, :].rearrange("p (k t) -> p k t", k=KT) for t in (h_hi, h_lo))
        WS = [[wsplit[:, (2 * b + part) * D:(2 * b + part + 1) * D].rearrange("p (k n) -> p k n", k=KT)
               for part in range(2)] for b in range(NSPLIT)]
        M = V(4096, KT, TT)
        Q = V(8192, KT, TT)
        K = V(12288, KT, TT)
        VV = V(16384, 4, D)
        U = V(20480, 4, 2, S + TAPS - 1)
        UC = V(22768, 4, TT)
        PL = V(24816, 4, 2, S + 16)
        PR = V(4096, 2, 2, 2, 512)
        GR = V(12288, 4, TT)
        PA = V(14336, 2, S + 16)
        PB = V(14880, 2, S + 16)
        PO = V(16384, 4, TT)
        FA = V(8192, FT, TT)

        consts_in, x_in, rows_in, dist_in = (sem(n) for n in ("consts_in", "x_in", "rows_in", "dist_in"))
        moe_consts_in, poolw_in, out_written, bd_in = (
            sem(n) for n in ("moe_consts_in", "poolw_in", "out_written", "bd_in"))
        chunk_full = [sem(f"chunk_full{s}") for s in range(NSLOT)]
        chunk_part_read = sem("chunk_part_read")
        mod_free = sem("mod_free")
        convolved, q_padded, pad_zeroed, rs_set = (
            sem(n) for n in ("convolved", "q_padded", "pad_zeroed", "rs_set"))
        w_hi, w_lo = sem("w_hi"), sem("w_lo")
        h_hi_set, h_lo_set = sem("h_hi_set"), sem("h_lo_set")
        pe_job = sem("pe_job")
        bank_free = [sem(f"bank_free{b}") for b in range(BANKS)]
        dve_chain, act_chain, pool_chain = sem("dve_chain"), sem("act_chain"), sem("pool_chain")
        ones_set, bd_zeroed, silu_sig, silu_set = (sem(n) for n in ("ones_set", "bd_zeroed", "silu_sig", "silu_set"))
        ada_set, squared, scaled, h_set, x_set = (
            sem(n) for n in ("ada_set", "squared", "scaled", "h_set", "x_set"))
        sp_abs, sp_exp, sp_one, sp_ln, sp_set = (sem(n) for n in ("sp_abs", "sp_exp", "sp_one", "sp_ln", "sp_set"))
        q_bias_set, conv1_set, decay_set, rnn_set = (
            sem(n) for n in ("q_bias_set", "conv1_set", "decay_set", "rnn_set"))
        max_set, prob_set, prob_normed, merged = (
            sem(n) for n in ("max_set", "prob_set", "prob_normed", "merged"))
        rmax_set, rexp_set, gate_set, mask_set, pos_set, lists_set, ff_done = (
            sem(n) for n in ("rmax_set", "rexp_set", "gate_set", "mask_set", "pos_set", "lists_set", "ff_done"))
        moe_full = [sem(f"moe_full{s}") for s in range(NSLOT)]
        over_full = [sem(f"over_full{s}") for s in range(OSLOT)]
        moe_read = sem("moe_read")
        gathered, gate_turned, act_turned, scattered = (
            sem(n) for n in ("gathered", "gate_turned", "act_turned", "scattered"))
        sel_set, glu_set, lin_set, half_act, act_set, added0, added1 = (
            sem(n) for n in ("sel_set", "glu_set", "lin_set", "half_act", "act_set", "added0", "added1"))
        xe_set, pgt_set, sig_set, at_set, ye_set = (
            sem(n) for n in ("xe_set", "pgt_set", "sig_set", "at_set", "ye_set"))
        lam_prod, rotated, heads_normed, centred, conv_scaled, conv_act, pooled = (
            sem(n) for n in ("lam_prod", "rotated", "heads_normed", "centred", "conv_scaled", "conv_act", "pooled"))
        eps_set, mult_set = sem("eps_set"), sem("mult_set")
        b2_zeroed, gatet_zeroed = sem("b2_zeroed"), sem("gatet_zeroed")
        b1_zeroed = sem("b1_zeroed")

        mod_done = {}
        rms_buffer = {}
        moe_base = []
        jobs = {}
        chunks = []
        release = []
        splits = []
        value_tile = {}
        step_start = {}
        jobs_to_free = {}
        chunk_at = []
        sq_release = []
        counts = {}

        def count(s, k=1):
            counts[id(s)] = counts.get(id(s), 0) + k
            return counts[id(s)]

        def bank(name):
            return ps[jobs[name] % BANKS]

        def job_done(eng, name):
            eng.wait_ge(pe_job, jobs[name] + 1)

        def bank_signal(name):
            return bank_free[jobs[name] % BANKS], jobs[name] // BANKS + 1

        def evacuated(eng, name):
            s, v = bank_signal(name)
            eng.wait_ge(s, v)

        def flat(v):
            return v.rearrange("p a b -> p (a b)")

        def parts_of(lo):
            return [(0, S, 1), (S, TT, 0)] if lo == 0 else [(S, TT, 0)]

        def segments(ap):
            return ap.rearrange("p (s t) -> p s t", t=S)

        class Next:

            def __init__(self, eng):
                self.eng, self.n = eng, {}

            def __call__(self, s, k=1):
                self.n[id(s)] = self.n.get(id(s), 0) + k
                self.eng.wait_ge(s, self.n[id(s)])

        def split_pair(j, part):
            b = sorted((j % NSPLIT, (j + 1) % NSPLIT))
            v = wsplit[:, :].rearrange("p (b s k n) -> p b s k n", b=NSPLIT, s=2, k=KT)
            return v[:, b[0]:b[1] + 1:b[1] - b[0], part]

        def weights_of(c):
            s = chunk_at[c][0]
            return ring2[:, s * SLOTW:(s + 1) * SLOTW].rearrange("p (k n) -> p k n", k=KT)

        block = ctx.enter_context(nc.Block())

        @block.tensor
        def _(pe):
            full = [0] * NSLOT

            def open_job(name):
                n = len(jobs)
                jobs[name] = n
                if n >= BANKS:
                    pe.wait_ge(bank_free[n % BANKS], n // BANKS)
                return ps[n % BANKS]

            def next_chunk(*loads):
                b = len(chunks) - moe_base[0] if moe_base else None
                s = len(chunks) % NSLOT if b is None else b % NSLOT2
                chunks.append(loads)
                release.append(None)
                full[s] += 16 * len(loads)
                chunk_at.append((s, full[s]))
                return s

            def take_chunk(*loads):
                s = next_chunk(*loads)
                pe.wait_ge(chunk_full[s], full[s])
                return (ring2 if moe_base else ring)[:, s * SLOTW:(s + 1) * SLOTW]

            def split_chunk(*loads):
                next_chunk(*loads)
                for col in range(2):
                    splits.append([len(chunks) - 1, col, None])
                release[-1] = (w_lo, len(splits))
                return len(splits) - 2

            def split_linear(name, j, c0=0, before=None):
                pe.wait_ge(w_lo, j + 1)
                hi, lo = WS[j % NSPLIT]
                o = open_job(name)
                for k in range(KT):
                    if before is not None:
                        pe.wait_ge(h_lo_set, before + k + 1)
                    for i, (w, h) in enumerate(((hi, HH), (hi, HL), (lo, HH))):
                        mm = pe.matmul(o[:, 0:TT - c0], w[:, k, :], h[:, k, c0:TT],
                                       start=(k == 0 and i == 0), stop=(k == KT - 1 and i == 2))
                mm.then_inc(pe_job, 1)
                splits[j][2] = len(jobs)

            def chunk_read_with_job(i=-1):
                release[i] = (pe_job, len(jobs))
                jobs_to_free[len(chunks) - 1] = len(jobs)

            def chunk_read_inside(mm):
                mm.then_inc(chunk_part_read, 1)
                release[-1] = (chunk_part_read, count(chunk_part_read))
                jobs_to_free[len(chunks) - 1] = len(jobs)

            def tiles(w_ap, c0, n=2, rows=D):
                return w_ap[:, c0:c0 + 128 * n].rearrange("(k p) n -> p k n", p=128), rows * n

            def linear(names, w, kt, rhs):
                wv = w[:, 0:kt * 128 * len(names)].rearrange("p (k n) -> p k n", k=kt)
                for i, name in enumerate(names):
                    o = open_job(name)
                    for k in range(kt):
                        mm = pe.matmul(o[:, 0:rhs(k).shape[-1]], wv[:, k, i * 128:(i + 1) * 128], rhs(k),
                                       start=(k == 0), stop=(k == kt - 1))
                    mm.then_inc(pe_job, 1)
                chunk_read_with_job()

            def mod_chunk(n, q, k):
                o, w_ap = ps[MODBANK], a["w_ada"] if n == 0 else a["w_mod_2"][n - 1]
                if k == 0:
                    pe.wait_ge(mod_free, 3 * n + q)
                w = take_chunk((w_ap[k * 128:(k + 1) * 128, q * SLOTW:(q + 1) * SLOTW], SLOTW))
                for j in range(4):
                    mm = pe.matmul(o[32 * j:32 * j + 32, :], CS[:, k, :], w[:, j * 512:(j + 1) * 512],
                                   start=(k == 0), stop=(k == KT - 1))
                chunk_read_inside(mm)
                mod_done[n, q] = release[-1]

            def mod_columns(n, q):
                pe.wait_ge(mod_free, 3 * n + q + 1)
                o = open_job(f"adaT{n}.{q}")
                for s in range(4):
                    mm = pe.transpose(o[:, s * 128:(s + 1) * 128], ADR[:, s * 128:(s + 1) * 128], ident)
                mm.then_inc(pe_job, 1)

            def square_sum(name, n, width):
                o = open_job(name)
                for t in range(n):
                    m = len(sq_release)
                    pe.wait_ge(squared, m + 1)
                    mm = pe.matmul(o[:, 0:width], ones[:, :], SQ[:, m % 2, 0:width], start=(t == 0), stop=(t == n - 1))
                    if t < n - 1:
                        mm.then_inc(chunk_part_read, 1)
                        sq_release.append((chunk_part_read, count(chunk_part_read)))
                mm.then_inc(pe_job, 1)
                sq_release.append((pe_job, len(jobs)))
                rms_buffer[name] = len(rms_buffer) % 2

            def block1():
                square_sum("b1.pre", KT, S)
                for k in range(KT):
                    mod_chunk(0, 0, k)
                mod_columns(0, 0)
                start = {"xr": 0, "gr": 1024, "q": 2048, "sr": 3584, "sa": 4608}
                chunk_no = {}

                def projection(part, t):
                    w_ap, c0, rhs = a["w_in"], start.get(part, 0), H1
                    if part in ("yr", "ya"):
                        w_ap, rhs = (a["w_o_rnn"], GG) if part == "yr" else (a["w_o_attn"], Q1)
                    if t % 2 == 0:
                        chunk_no[part] = len(chunks)
                        chunk_no[part, "w"] = take_chunk(tiles(w_ap, c0 + 128 * t))
                    w = chunk_no[part, "w"].rearrange("p (k n) -> p k n", k=KT)
                    o = open_job(f"{part}{t}")
                    for k in range(KT):
                        if part == "xr" and t == 0:
                            pe.wait_ge(h_set, k + 1)
                        mm = pe.matmul(o[:, 0:S], w[:, k, (t % 2) * 128:(t % 2) * 128 + 128], rhs[:, k, :],
                                       start=(k == 0), stop=(k == KT - 1))
                    mm.then_inc(pe_job, 1)
                    release[chunk_no[part]] = (pe_job, len(jobs))

                for step in block1_steps():
                    kind = step[0]
                    if kind == "lin":
                        if step[1:] == ("yr", 0):
                            pe.wait_ge(rnn_set, 1)
                        if step[1:] == ("ya", 0):
                            evacuated(pe, "o15")
                        projection(*step[1:])
                    elif kind == "mod":
                        mod_chunk(*step[1:])
                    elif kind == "modT":
                        mod_columns(*step[1:])
                    elif kind == "gates":
                        pe.wait_ge(bd_in, 64)
                        pe.wait_ge(conv1_set, 1)
                        for part, b in (("ga", 0), ("gi", 1)):
                            for t in range(KT):
                                o = open_job(f"{part}{t}")
                                pe.matmul(o[:, 0:S], BD[:, b, t, :], XC[:, t, :], start=True, stop=True)\
                                    .then_inc(pe_job, 1)
                    elif kind == "k":
                        w = take_chunk(tiles(a["w_in"], 3072))
                        wv = w.rearrange("p (k n) -> p k n", k=KT)
                        for g in range(4):
                            o = open_job(f"k{g}")
                            for k in range(KT):
                                for p0 in (0, 64):
                                    mm = pe.matmul(o[p0:p0 + 64, 0:S], wv[:, k, 64 * g:64 * g + 64],
                                                   H1[:, k, :], start=(k == 0), stop=(k == KT - 1))
                            mm.then_inc(pe_job, 1)
                        chunk_read_with_job()
                    elif kind == "v":
                        w = take_chunk(tiles(a["w_in"], 3328))
                        wv = w.rearrange("p (k n) -> p k n", k=KT)
                        pe.wait_ge(rows_in, 16)
                        for i in range(2):
                            o = open_job(f"v{i}")
                            for k in range(KT):
                                pe.matmul(o[:, 0:256], H1[:, k, 128 * i:128 * i + 128], wv[:, k, :],
                                          start=(k == 0), stop=False)
                            pe.matmul(o[:, 0:256], ones[0:1, :], ROWS[0:1, 0:256], start=False, stop=True)\
                                .then_inc(pe_job, 1)
                        chunk_read_with_job()
                    elif kind == "S":
                        hd = step[1]
                        if hd == 0:
                            evacuated(pe, "k3")
                            evacuated(pe, "v1")
                        pe.wait_ge(q_padded, hd + 1)
                        g, z = hd // 4, SQ[:, hd % 2, 0:S]
                        o = open_job(f"s{hd}")
                        pe.matmul(o[:, 0:128], z[:, 0:128], K1[:, g, 0:128], start=True, stop=True)
                        pe.matmul(o[:, 128:384], z[:, 128:256], K1[:, g, :], start=True, stop=True)\
                            .then_inc(pe_job, 1)
                    elif kind == "T":
                        hd = step[1]
                        pe.wait_ge(prob_normed, hd + 1)
                        o = open_job(f"pt{hd}")
                        for j in range(3):
                            mm = pe.transpose(o[:, j * 128:(j + 1) * 128], P1[:, hd % 2, j * 128:(j + 1) * 128], ident)
                        mm.then_inc(pe_job, 1)
                    elif kind == "O":
                        hd = step[1]
                        p0, g = 64 * (hd % 2), hd // 4
                        evacuated(pe, f"pt{hd}")
                        o = open_job(f"o{hd}")[p0:p0 + 64, :]
                        pe.matmul(o[:, 0:128], V1[:, 0, 64 * g:64 * g + 64], PT1[:, hd % 2, 0:128],
                                  start=True, stop=True)
                        for j in range(2):
                            mm = pe.matmul(o[:, 128:256], V1[:, j, 64 * g:64 * g + 64],
                                           PT1[:, hd % 2, 128 * (j + 1):128 * (j + 2)], start=(j == 0), stop=(j == 1))
                        mm.then_inc(pe_job, 1)
                pe.wait_ge(merged, KT)
                for c in range(4):
                    w = take_chunk(tiles(a["w_out"], 256 * c))
                    linear([f"mx{2 * c}", f"mx{2 * c + 1}"], w, KT, lambda k: M1[:, k, :])
                square_sum("b1.post", KT, S)
                square_sum("b1.ffn", KT, S)

            def gather(gi, par):
                pe.wait_ge(sel_set, gi[0])
                for ft in range(KT):
                    for i in range(2):
                        mm = pe.matmul(ps[2][:, ft * SLOT:(ft + 1) * SLOT], HT[:, i, ft * 128:(ft + 1) * 128],
                                       PSEL[:, i, 0:SLOT], start=(i == 0), stop=(i == 1))
                mm.then_inc(gathered, 1)
                for half in range(2):
                    for i in range(2):
                        mm = pe.transpose(ps[3][:, half * S + i * 128:half * S + (i + 1) * 128],
                                          GSEL[:, i, half, :], ident)
                mm.then_inc(gate_turned, 1)

            def hidden(n, gi, par, slot_of, full_wait):
                pe.wait_ge(xe_set, gi + 1)
                pe.wait_ge(pgt_set, gi + 1)
                pe.wait_ge(added0, n)
                for b in range(2):
                    for p0 in (0, 64):
                        c0 = D * (p0 // 64) + 512 * b
                        pe.matmul(ps[b][p0:p0 + 64, :], BSEL[:, par, :], B1[:, c0:c0 + 512], start=True, stop=False)
                for k in range(KT):
                    full_wait(k)
                    w = ring[:, slot_of(k) * SLOTW:(slot_of(k) + 1) * SLOTW]
                    for b in range(2):
                        for p0 in (0, 64):
                            c0 = D * (p0 // 64) + 512 * b
                            mm = pe.matmul(ps[b][p0:p0 + 64, :], XE[:, k, :], w[:, c0:c0 + 512],
                                           start=False, stop=(k == KT - 1))
                    mm.then_inc(moe_read, 1)

            def down(n, par, slot_of, full_wait):
                pe.wait_ge(act_set, n + 1)
                for j in range(4):
                    mm = pe.transpose(ps[4][:, j * 128:(j + 1) * 128], AC[:, j * 128:(j + 1) * 128], ident)
                mm.then_inc(act_turned, 1)
                pe.wait_ge(at_set, n + 1)
                for k in range(KT):
                    c = KT + k // 2
                    if k % 2 == 0:
                        full_wait(c)
                    w = ring[:, slot_of(c) * SLOTW + D * (k % 2):slot_of(c) * SLOTW + D * (k % 2) + D]
                    for p0 in (0, 64):
                        c0 = 512 * (p0 // 64)
                        mm = pe.matmul(ps[5][p0:p0 + 64, :], AT[:, k % 4, 64 * (k // 4):64 * (k // 4) + 64],
                                       w[:, c0:c0 + 512], start=(k == 0), stop=(k == KT - 1))
                    if k % 2:
                        mm.then_inc(moe_read, 1)

            def scatter(n, gi, par):
                pe.wait_ge(ye_set, n + 1)
                for r in range(2):
                    if r:
                        pe.wait_ge(added1, n)
                    for f in range(2):
                        for half in range(2):
                            mm = pe.matmul(ps[(0, 6)[r] + half][:, f * S:(f + 1) * S],
                                           YE[:, (2 * r + f) * 128:(2 * r + f + 1) * 128],
                                           PGT[:, par, half, :], start=True, stop=True)
                    mm.then_inc(scattered, 1)

            def moe():
                pe.wait_ge(moe_consts_in, 16 * 4)
                pe.wait_ge(h_set, 2 * KT)
                for i in range(2):
                    o = open_job(f"lg{i}")
                    for k in range(KT):
                        pe.matmul(o[:, 0:NE], H2[:, k, 128 * i:128 * i + 128], RW[:, k, :], start=(k == 0), stop=False)
                    pe.matmul(o[:, 0:NE], ones[0:1, :], ROWS[0:1, S:S + NE], start=False, stop=True)\
                        .then_inc(pe_job, 1)
                for i in range(2):
                    for half in range(2):
                        o = open_job(f"ht{i}{half}")
                        for j in range(4):
                            mm = pe.transpose(o[:, j * 128:(j + 1) * 128],
                                              H2[:, 4 * half + j, 128 * i:128 * i + 128], ident)
                        mm.then_inc(pe_job, 1)
                pe.wait_ge(mask_set, 2)
                for i in range(2):
                    o = open_job(f"pos{i}")
                    if i:
                        pe.matmul(o[:, 0:NE], ones[:, :], MK[:, 0, :], start=True, stop=False)
                    pe.matmul(o[:, 0:NE], before, MK[:, i, :], start=(i == 0), stop=True).then_inc(pe_job, 1)
                o = open_job("cnt")
                for i in range(2):
                    mm = pe.matmul(o[:, 0:NE], ones[:, :], MK[:, i, :], start=(i == 0), stop=(i == 1))
                mm.then_inc(pe_job, 1)
                pe.wait_ge(gate_set, 2)
                o = open_job("gt")
                for i in range(2):
                    mm = pe.transpose(o[0:NE, i * 128:(i + 1) * 128], GATE[:, i, 0:NE], ident)
                mm.then_inc(pe_job, 1)
                pe.wait_ge(gatet_zeroed, 1)
                evacuated(pe, "gt")
                for j in range(4):
                    o = open_job(f"b2{j}")
                    for f in range(2):
                        mm = pe.matmul(o[:, f * S:(f + 1) * S], B2[:, (2 * j + f) * 128:(2 * j + f + 1) * 128],
                                       GATET, start=True, stop=True)
                    mm.then_inc(pe_job, 1)
                for name in list(jobs)[-BANKS:]:
                    evacuated(pe, name)
                pe.wait_ge(mod_free, 6 if "a" in phases else 0)
                base = len(chunks)
                gather([1], 0)
                with pe.Fori(0, NE // 2) as it:
                    for u in range(2):
                        n = it * 2 + u

                        def full_wait(c, it=it, u=u):
                            j = EC * u + c
                            pe.wait_ge(moe_full[(base + j) % NSLOT], it * 48 + 16 * (j // NSLOT + 1))

                        def slot_of(c, u=u):
                            return (base + EC * u + c) % NSLOT

                        hidden(n, n, u, slot_of, full_wait)
                        gather([n + 2], 1 - u)
                        down(n, u, slot_of, full_wait)
                        scatter(n, n, u)
                moe_base.append(base)
                pe.wait_ge(lists_set, 1)
                n_over = pe.value_load(lists[0:1, 2 * OVERMAX:2 * OVERMAX + 1], min_val=0, max_val=OVERMAX)
                with pe.If(n_over > 0):
                    with pe.Fori(0, n_over) as q:
                        n = q + NE

                        def full_wait(c, q=q):
                            pe.wait_ge(over_full[c % OSLOT], q * 32 + 16 * (c // OSLOT + 1))

                        gather([q + (NE + 3)], 0)
                        hidden(n, q + (NE + 1), 0, lambda c: c % OSLOT, full_wait)
                        down(n, 0, lambda c: c % OSLOT, full_wait)
                        scatter(n, q + (NE + 1), 0)
                with pe.Else():
                    pass
                square_sum("b1.out", KT, S)

            def layer(l):
                lo = 0 if l == 0 else S
                w_in = a["w_in_2"][l]
                width = TT - lo
                square_sum(f"pre{l}", KT, TT)
                groups = groups_of(l)
                start = {"lg": 512, "la": 0, "q": 1024, "k": 2048, "p": 4096}
                held = {}

                def split_job(name, key, t, load, c0, before=None):
                    if t % 2 == 0:
                        held[key] = split_chunk(load(t))
                    split_linear(name, held[key] + t % 2, c0, before)

                def job(name, key, t, per, load, kt, view, lo):
                    if t % per == 0:
                        held[key] = (len(chunks), take_chunk(load(t)))
                    c, w = held[key]
                    w = w.rearrange("p (k n) -> p k n", k=kt)
                    o = open_job(name)
                    for k in range(kt):
                        mm = pe.matmul(o[:, 0:TT - lo], w[:, k, (t % per) * 128:(t % per) * 128 + 128],
                                       view[:, k, lo:TT], start=(k == 0), stop=(k == kt - 1))
                    mm.then_inc(pe_job, 1)
                    release[c] = (pe_job, len(jobs))
                    jobs_to_free[c] = len(jobs)

                y_of = {0: ("w_conv_out_2", UC, 4), 1: ("w_attn_out_2", Q, 8), 2: ("w_pool_out_2", PO, 4)}
                for at, step in enumerate(layer_steps(l)):
                    kind = step[0]
                    step_start[l, at] = len(jobs)
                    if kind == "lin":
                        part, t = step[1:]
                        split_job(f"{part}{l}.{t}", part, t, lambda t: tiles(w_in, start[part] + 128 * t),
                                  0 if part == "k" else lo, KT * 2 * l if (part, t) == ("lg", 0) else None)
                    elif kind == "mod":
                        mod_chunk(*step[1:])
                    elif kind == "modT":
                        mod_columns(*step[1:])
                    elif kind == "v":
                        c, i = step[1:]
                        if i == 0:
                            held["v"] = value_tile[l, c] = split_chunk(tiles(w_in, 3072 + 256 * c))
                        pe.wait_ge(w_lo, held["v"] + 2)
                        o = open_job(f"v{l}.{c}.{i}")
                        hi, lo_w = (split_pair(held["v"], part) for part in range(2))
                        for ii in range(2):
                            tok = slice((i + ii) * 128, (i + ii + 1) * 128)
                            for k in range(KT):
                                for n, (h, w) in enumerate(((HH, hi), (HH, lo_w), (HL, hi))):
                                    mm = pe.matmul(o[:, ii * 256:ii * 256 + 256], h[:, k, tok], w[:, :, k, :],
                                                   start=(k == 0 and n == 0), stop=(k == KT - 1 and n == 2))
                        mm.then_inc(pe_job, 1)
                        for half in range(2):
                            splits[held["v"] + half][2] = len(jobs)
                    elif kind == "rot":
                        c = step[1]
                        for t in (2 * c, 2 * c + 1):
                            for part, view in (("q", Q), ("k", K)):
                                evacuated(pe, f"{part}{l}.{t}")
                                o = open_job(f"rot{part}{l}.{t}")
                                pe.matmul(o[:, 0:S], rot, view[:, t, S:TT], start=True, stop=True)\
                                    .then_inc(pe_job, 1)
                        if c == 0:
                            pe.wait_ge(lam_prod, l + 1)
                            o = open_job(f"lam{l}")
                            pe.matmul(o[:, 0:2], ones[:, :], LAMP, start=True, stop=True).then_inc(pe_job, 1)
                    elif kind == "S":
                        gi = step[1]
                        hd, blocks, nk = groups[gi]
                        pe.wait_ge(rotated, 4 * l + hd // 2 + 1)
                        pe.wait_ge(q_padded, 16 + 16 * l + gi + 1)
                        for j, b in enumerate(blocks):
                            for comp in range(2):
                                o = open_job(f"s{l}.{gi}.{b}.{comp}")
                                z = SQ[:, gi % 2, comp * S + j * 128:comp * S + (j + 1) * 128]
                                pe.matmul(o[:, 0:nk], z, K[:, hd, 0:nk], start=True, stop=True).then_inc(pe_job, 1)
                    elif kind == "T":
                        gi = step[1]
                        hd, blocks, nk = groups[gi]
                        for j, b in enumerate(blocks):
                            pe.wait_ge(prob_normed, 16 + 32 * l + 2 * gi + j + 1)
                            o = open_job(f"pt{l}.{gi}.{b}")
                            for k in range(nk // 128):
                                mm = pe.transpose(o[:, k * 128:(k + 1) * 128],
                                                  PR[:, gi % 2, j, 0, k * 128:(k + 1) * 128], ident)
                            mm.then_inc(pe_job, 1)
                    elif kind == "O":
                        gi = step[1]
                        hd, blocks, nk = groups[gi]
                        evacuated(pe, f"v{l}.{hd // 2}.2")
                        for b in blocks:
                            evacuated(pe, f"pt{l}.{gi}.{b}")
                        o = open_job(f"o{l}.{gi}")
                        for k in range(nk // 128):
                            mm = pe.matmul(o[:, 0:S], VV[:, k, hd * 128:(hd + 1) * 128],
                                           PR[:, gi % 2, :, 1, k * 128:(k + 1) * 128],
                                           start=(k == 0), stop=(k == nk // 128 - 1))
                        mm.then_inc(pe_job, 1)
                    elif kind == "mean":
                        pe.wait_ge(convolved, 4 * (l + 1))
                        o = open_job(f"mean{l}")
                        for t in range(4):
                            mm = pe.matmul(o[:, 0:width], ones[:, :], UC[:, t, lo:TT], start=(t == 0), stop=(t == 3))
                        mm.then_inc(pe_job, 1)
                    elif kind == "var":
                        square_sum(f"var{l}", 4, width)
                    elif kind == "sub":
                        square_sum(f"sub{l}.{step[1]}", 1, width)
                    elif kind == "gate":
                        br, t = step[1:]
                        split_job(f"g{l}.{br}.{t}", "gate", t, lambda t: tiles(w_in, 4608 + D * br + 128 * t), lo)
                    elif kind == "mix":
                        pe.wait_ge(poolw_in, 16 * (l + 1))
                        for t in range(4):
                            pe.wait_ge(pooled, 4 * l + t + 1)
                            o = open_job(f"pm{l}.{t}")
                            pe.matmul(o[:, 0:width], POOLW[:, t, :], PO[:, t, lo:TT], start=True, stop=True)\
                                .then_inc(pe_job, 1)
                    elif kind == "y":
                        br, t = step[1:]
                        wy, view, kt = y_of[br]
                        per = 16 // kt
                        if t == 0:
                            if br == 0:
                                pe.wait_ge(conv_act, 4 * (l + 1))
                            elif br == 1:
                                pe.wait_ge(heads_normed, KT * (l + 1))
                            else:
                                for i in range(4):
                                    evacuated(pe, f"pm{l}.{i}")
                        job(f"y{l}.{br}.{t}", "y", t, per, lambda t: tiles(a[wy][l], 128 * t, per, 128 * kt), kt,
                            view, lo)
                pe.wait_ge(merged, KT * (l + 2))
                for c in range(4):
                    w = take_chunk(tiles(a["w_out_2"][l], 256 * c))
                    linear([f"m{l}.{2 * c}", f"m{l}.{2 * c + 1}"], w, KT, lambda k: M[:, k, lo:TT])
                square_sum(f"post{l}", KT, width)
                square_sum(f"ffn{l}", KT, width)
                w1 = a["w_ffn_in_2"][l]
                for c in range(HALF):
                    for part, c0 in (("fg", 0), ("fu", DFF)):
                        j = split_chunk(tiles(w1, c0 + 256 * c))
                        for i in range(2):
                            split_linear(f"{part}{l}.{2 * c + i}", j + i, lo,
                                         KT * (2 * l + 1) if (part, c, i) == ("fg", 0, 0) else None)
                evacuated(pe, f"fu{l}.{FT - 2}")
                evacuated(pe, f"fu{l}.{FT - 1}")
                w2 = a["w_ffn_out_2"][l]
                for t in range(KT):
                    o = open_job(f"f{l}.{t}")
                    for half in range(2):
                        src = w2[half * HALF * 128:(half + 1) * HALF * 128, t * 128:(t + 1) * 128]
                        w = take_chunk((src.rearrange("(k p) n -> p k n", p=128), HALF * 128))
                        wv = w[:, 0:HALF * 128].rearrange("p (k n) -> p k n", k=HALF)
                        for k in range(HALF):
                            mm = pe.matmul(o[:, 0:width], wv[:, k, :], FA[:, half * HALF + k, lo:TT],
                                           start=(half == 0 and k == 0), stop=(half == 1 and k == HALF - 1))
                        if half == 0:
                            chunk_read_inside(mm)
                    mm.then_inc(pe_job, 1)
                    chunk_read_with_job()
                square_sum(f"out{l}", KT, width)

            pe.wait_ge(ones_set, 1)
            pe.wait_ge(consts_in, 32)
            pe.wait_ge(silu_set, 1)
            if "a" in phases:
                block1()
            if "b" in phases:
                moe()
            if "c" in phases:
                for l in range(LAYERS):
                    layer(l)


        @block.sync
        def _(sp):
            sp.dma_start(cols[:, :], a["cols"]).then_inc(consts_in, 16)
            sp.dma_start(kept[:, :], a["kept"]).then_inc(consts_in, 16)
            sp.dma_start(X[:, :, S:TT], a["x"].rearrange("(k p) t -> p k t", p=128)).then_inc(x_in, 16)

            def slot_view(ring, s, src, at, n):
                v = ring[:, s * SLOTW + at:s * SLOTW + at + n]
                return v.rearrange("p (k n) -> p k n", k=src.shape[1]) if len(src.shape) == 3 else v

            def ordinary(c, n_over=0):
                slot = chunk_at[c][0]
                later = moe_base and c >= moe_base[0]
                if later and c < moe_base[0] + NSLOT2:
                    sp.wait_ge(moe_read, n_over * EC + EC * NE)
                elif later or c >= NSLOT:
                    s, v = release[c - (NSLOT2 if later else NSLOT)]
                    sp.wait_ge(s, v)
                at = 0
                for src, n in chunks[c]:
                    sp.dma_start(slot_view(ring2 if later else ring, slot, src, at, n), src)\
                        .then_inc(chunk_full[slot], 16)
                    at += n

            def expert_chunk(e, c):
                if c < KT:
                    return a["moe_w1"][bass.ds(e, 1), c * 128:(c + 1) * 128, :].rearrange("a p n -> p (a n)")
                r = (c - KT) * 256
                return a["moe_w2"][bass.ds(e, 1), r:r + 256, :].rearrange("a (k p) n -> p (a k) n", p=128)

            def load_expert(e, c, s, full):
                src = expert_chunk(e, c)
                sp.dma_start(slot_view(ring, s, src, 0, SLOTW), src).then_inc(full, 16)

            n_over = 0
            n_before = moe_base[0] if moe_base else len(chunks)
            for c in range(n_before):
                ordinary(c)
                if c == 8:
                    sp.dma_start(X[:, :, 0:S], a["ctx"].rearrange("(k p) t -> p k t", p=128)).then_inc(x_in, 16)
            if moe_base:
                base = moe_base[0]

                def load(it, g):
                    s = (base + g) % NSLOT
                    load_expert(it * 2 + g // EC, g % EC, s, moe_full[s])

                for g in range(NSLOT):
                    s, v = release[base + g - NSLOT]
                    sp.wait_ge(s, v)
                    load(0, g)
                with sp.Fori(0, NE // 2 - 1) as it:
                    for m in range(2 * EC):
                        sp.wait_ge(moe_read, it * (2 * EC) + m + 1)
                        load(it, NSLOT + m)
                for m in range(2 * EC - NSLOT):
                    sp.wait_ge(moe_read, (NE // 2 - 1) * 2 * EC + m + 1)
                    load(NE // 2 - 1, NSLOT + m)
                sp.wait_ge(lists_set, 1)
                n_over = sp.value_load(lists[0:1, 2 * OVERMAX:2 * OVERMAX + 1], min_val=0, max_val=OVERMAX)
                with sp.If(n_over > 0):
                    sp.wait_ge(moe_read, EC * NE)
                    with sp.Fori(0, n_over) as q:
                        e = sp.value_load(lists[0:1, bass.ds(q, 1)], min_val=0, max_val=NE - 1)
                        for c in range(EC):
                            sp.wait_ge(moe_read, q * EC + (EC * NE - OSLOT + c + 1))
                            load_expert(e, c, c % OSLOT, over_full[c % OSLOT])
                with sp.Else():
                    pass
            for c in range(n_before, len(chunks)):
                ordinary(c, n_over)
            out_t = a["out"].rearrange("(k p) t -> p k t", p=128)
            sp.wait_ge(x_set, KT * (("a" in phases) + ("b" in phases) + 2 * LAYERS * ("c" in phases)))
            sp.dma_start(out_t, X[:, :, S:TT]).then_inc(out_written, 16)
            sp.wait_ge(out_written, 16)

        @block.gpsimd
        def _(pool):
            chain = [0]

            def link(ins):
                chain[0] += 1
                ins.then_inc(pool_chain, 1)
                pool.wait_ge(pool_chain, chain[0])

            pool.memset(ones[:, :], 1.0).then_inc(ones_set, 1)
            pool.memset(V(19992, 2 * KT * 128), 0.0).then_inc(bd_zeroed, 1)
            pool.dma_start(ROWS[0:1, :], a["rows"]).then_inc(rows_in, 16)
            pool.dma_start(DIST, a["dist"]).then_inc(dist_in, 16)
            pool.wait_ge(bd_zeroed, 1)
            for b, name in enumerate(("rg_w_a", "rg_w_x")):
                w = a[name].rearrange("(t h) i j -> h i t j", h=2)
                for half in range(2):
                    pool.dma_start(BD[64 * half:64 * half + 64, b, :, 64 * half:64 * half + 64], w[half])\
                        .then_inc(bd_in, 16)

            if "b" in phases:
                if "a" in phases:
                    pool.wait_ge(merged, KT)
                pool.memset(B1, 0.0).then_inc(b1_zeroed, 1)
                pool.memset(B2, 0.0).then_inc(b2_zeroed, 1)
                pool.memset(GATET, 0.0).then_inc(gatet_zeroed, 1)
                pool.dma_start(RW, a["router_w"].rearrange("(k p) e -> p k e", p=128)).then_inc(moe_consts_in, 16)
                pool.dma_start(RT, a["route"]).then_inc(moe_consts_in, 16)
                pool.wait_ge(b1_zeroed, 1)
                pool.wait_ge(b2_zeroed, 1)
                pool.dma_start(B2[0:NE, :], a["moe_b2"]).then_inc(moe_consts_in, 16)
                pool.dma_start(B1[0:NE, :], a["moe_b1"]).then_inc(moe_consts_in, 16)
            for j, (c, col, _) in enumerate(splits):
                pool.wait_ge(w_hi, j + 1)
                hi, lo = WS[j % NSPLIT]
                pool.tensor_tensor(lo, weights_of(c)[:, :, col * 128:col * 128 + 128], hi, SUB).then_inc(w_lo, 1)

        @block.scalar
        def _(act):
            nxt = Next(act)
            sq_at = [0]

            def evac(name, out, func=ACT.Copy, src=None, **kw):
                job_done(act, name)
                s, _ = bank_signal(name)
                act.activation(out, bank(name)[:, 0:out.shape[-1]] if src is None else src, func, **kw).then_inc(s, 1)

            def square(src):
                m = sq_at[0]
                sq_at[0] += 1
                if m >= 2:
                    act.wait_ge(*sq_release[m - 2])
                act.activation(SQ[:, m % 2, 0:src.shape[-1]], src, ACT.Square).then_inc(squared, 1)

            def root(name, width, n):
                v = RS[:, rms_buffer[name], 0:width]
                evac(name, v, ACT.Ln, bias=EPSC, scale=1.0 / n)
                evacuated(act, name)
                act.activation(v, v, ACT.Exp, scale=-0.5).then_inc(rs_set, 1)

            def shift(n, out, off, lo, first):
                for t in range(KT):
                    nxt(scaled)
                    for a0, b0, m in parts_of(lo):
                        i = act.activation(out[:, t, a0 - off:b0 - off], out[:, t, a0 - off:b0 - off], ACT.Identity,
                                           bias=ADA[:, n, m, first + t:first + t + 1])
                    i.then_inc(h_set, 1)

            def shift_hi(n, lo, first):
                for t in range(KT):
                    nxt(scaled)
                    for a0, b0, m in parts_of(lo):
                        i = act.activation(HH[:, t, a0:b0], M[:, t, a0:b0], ACT.Identity,
                                           bias=ADA[:, n, m, first + t:first + t + 1])
                    i.then_inc(h_hi_set, 1)

            split_at = [0]

            def split_ahead(n):
                while split_at[0] < len(splits):
                    j = split_at[0]
                    c, col, _ = splits[j]
                    if max(jobs_to_free.get(b, 0) for b in range(c - NSLOT2 + 1)) > n:
                        return
                    if j >= NSPLIT:
                        free = splits[j - NSPLIT][2]
                        if free > n:
                            return
                        act.wait_ge(pe_job, free)
                    s, v = chunk_at[c]
                    act.wait_ge(chunk_full[s], v)
                    act.activation(WS[j % NSPLIT][0], weights_of(c)[:, :, col * 128:col * 128 + 128], ACT.Copy)\
                        .then_inc(w_hi, 1)
                    split_at[0] += 1

            def mod_rows(n, q):
                act.wait_ge(*mod_done[n, q])
                if mod_parts.index((n, q)):
                    pn, pq = mod_parts[mod_parts.index((n, q)) - 1]
                    job_done(act, f"adaT{pn}.{pq}")
                act.activation(ADR, ps[MODBANK][:, :], ACT.Copy).then_inc(mod_free, 1)

            mod_parts = sorted(mod_done)

            def block1():
                al = SP[:, 0, :]
                nxt(sp_abs)
                act.activation(SP[:, 1, :], al, ACT.Exp, scale=-1.0).then_inc(sp_exp, 1)
                nxt(sp_one)
                act.activation(SP[:, 3, :], SP[:, 2, :], ACT.Ln).then_inc(sp_ln, 1)
                act.wait_ge(x_in, 16)
                for t in range(KT):
                    square(X[:, t, S:TT])
                act.wait_ge(eps_set, 1)
                root("b1.pre", S, D)
                mod_rows(0, 0)
                nxt(ada_set)
                shift(0, H1, S, S, 0)
                for step in block1_steps():
                    kind = step[0]
                    if kind == "lin":
                        part, t = step[1:]
                        if part == "xr":
                            evac(f"xr{t}", XR[:, t, 3:S + 3], ACT.Identity, bias=C("b_in", t))
                        elif part == "gr":
                            evac(f"gr{t}", GG[:, t, :], ACT.Gelu_apprx_tanh, bias=C("b_in", 8 + t))
                        elif part == "q":
                            if t == 0:
                                act.wait_ge(q_bias_set, 1)
                            evac(f"q{t}", Q1[:, t, :], ACT.Identity, bias=QB[:, t:t + 1], scale=0.125)
                        elif part == "sr":
                            evac(f"sr{t}", SR[:, t, :], ACT.Sigmoid, bias=C("b_in", 28 + t))
                        elif part == "sa":
                            evac(f"sa{t}", SA[:, t, :], ACT.Sigmoid, bias=C("b_in", 36 + t))
                    elif kind == "mod" and step[3] == KT - 1:
                        mod_rows(*step[1:3])
                    elif kind == "gates":
                        for part, buf, bias in (("ga", GA, "b_a"), ("gi", GI, "b_x")):
                            for t in range(KT):
                                evac(f"{part}{t}", buf[:, t, :], ACT.Sigmoid, bias=C(bias, t))
                        nxt(sp_set)
                        evacuated(act, "ga7")
                        for t in range(KT):
                            act.activation(MU[:, t, :], GA[:, t, :], ACT.Tanh, scale=P4[:, t:t + 1])\
                                .then_inc(act_chain, 1)
                        act.wait_ge(act_chain, count(act_chain, KT))
                        for t in range(KT):
                            act.activation(GA[:, t, :], GA[:, t, :], ACT.Exp, scale=K8[:, t:t + 1])\
                                .then_inc(decay_set, 1)
                        act.activation(flat(MU), flat(MU), ACT.Sqrt).then_inc(mult_set, 1)
                    elif kind == "k":
                        for g in range(4):
                            evac(f"k{g}", K1[:, g, :], ACT.Identity, bias=C("bk", g))
                    elif kind == "v":
                        for i in range(2):
                            evac(f"v{i}", V1[:, i, :])
                    elif kind == "Z":
                        hd = step[1]
                        p0 = 64 * (hd % 2)
                        if hd == 0:
                            act.wait_ge(pad_zeroed, 1)
                            evacuated(act, "q7")
                        if hd >= 2:
                            job_done(act, f"s{hd - 2}")
                        act.activation(SQ[p0:p0 + 64, hd % 2, 0:S], Q1[p0:p0 + 64, hd // 2, :], ACT.Copy)\
                            .then_inc(q_padded, 1)
                    elif kind == "S":
                        hd = step[1]
                        nxt(max_set)
                        st = ST1[:, hd % 2]
                        for b, (c0, c1) in enumerate(((0, 128), (128, 384))):
                            act.activation(P1[:, hd % 2, c0:c1], P1[:, hd % 2, c0:c1], ACT.Exp,
                                           bias=st[:, 1, b:b + 1], accum_out=st[:, 2, b:b + 1])
                        act.activation(st[:, 3, :], st[:, 1, :], ACT.Exp, bias=C("sinks", hd)).then_inc(prob_set, 1)
                    elif kind == "T":
                        evac(f"pt{step[1]}", PT1[:, step[1] % 2, :])
                    elif kind == "O":
                        hd = step[1]
                        p0 = 64 * (hd % 2)
                        evac(f"o{hd}", Q1[p0:p0 + 64, hd // 2, :], src=bank(f"o{hd}")[p0:p0 + 64, 0:S])
                for t in range(KT):
                    evac(f"mx{t}", MX1[:, t, :])
                    evacuated(act, f"mx{t}")
                    square(MX1[:, t, :])
                root("b1.post", S, D)
                for t in range(KT):
                    nxt(x_set)
                    square(X[:, t, S:TT])
                root("b1.ffn", S, D)
                shift(0, H2, S, S, 24)

            def xe_evac():
                act.activation(XE, ps[2][:, :].rearrange("p (k m) -> p k m", k=KT), ACT.Copy).then_inc(xe_set, 1)

            def pgt_evac(par):
                act.activation(PGT[:, par, :, :], ps[3][:, :].rearrange("p (h t) -> p h t", h=2), ACT.Copy)\
                    .then_inc(pgt_set, 1)

            def gathers(gi, par):
                act.wait_ge(gathered, gi)
                xe_evac()
                act.wait_ge(gate_turned, gi)
                pgt_evac(par)

            def sigmoids(n):
                act.wait_ge(glu_set, n + 1)
                act.activation(SIG, GLU, ACT.Sigmoid, scale=ALPHA).then_inc(sig_set, 1)

            def rest(n, read):
                act.wait_ge(act_turned, n + 1)
                act.activation(AT, ps[4][:, :].rearrange("p (k m) -> p k m", k=4), ACT.Copy).then_inc(at_set, 1)
                act.wait_ge(moe_read, read)
                act.activation(YE, ps[5][:, :], ACT.Copy).then_inc(ye_set, 1)

            def moe():
                for i in range(2):
                    for half in range(2):
                        evac(f"ht{i}{half}", HT[:, i, 512 * half:512 * half + 512])
                for i in range(2):
                    nxt(rmax_set)
                    act.activation(EX[:, i, :], LG[:, i, 0:NE], ACT.Exp, bias=GST[:, i, 0:1]).then_inc(rexp_set, 1)
                job_done(act, "gt")
                act.wait_ge(gatet_zeroed, 1)
                s, _ = bank_signal("gt")
                act.activation(GATET[0:NE, :], bank("gt")[0:NE, 0:S], ACT.Copy).then_inc(s, 1)
                gathers(1, 0)
                with act.Fori(0, NE // 2) as it:
                    for u in range(2):
                        n = it * 2 + u
                        sigmoids(n)
                        gathers(n + 2, 1 - u)
                        rest(n, it * (2 * EC) + EC * (u + 1))
                act.wait_ge(lists_set, 1)
                n_over = act.value_load(lists[0:1, 2 * OVERMAX:2 * OVERMAX + 1], min_val=0, max_val=OVERMAX)
                with act.If(n_over > 0):
                    with act.Fori(0, n_over) as q:
                        gathers(q + (NE + 2), 0)
                        sigmoids(q + NE)
                        rest(q + NE, q * EC + EC * (NE + 1))
                with act.Else():
                    pass
                act.wait_ge(ff_done, 1)
                for t in range(KT):
                    square(FF[:, t, :])
                root("b1.out", S, D)

            def layer(l):
                lo = 0 if l == 0 else S
                s0 = lo // S
                act.wait_ge(x_in, 32)
                for t in range(KT):
                    nxt(x_set)
                    square(X[:, t, :])
                root(f"pre{l}", TT, D)
                split_ahead(jobs[f"pre{l}"] + 1)
                shift_hi(1 + l, 0, 0)
                groups = groups_of(l)
                ring_user = []
                for at, step in enumerate(layer_steps(l)):
                    kind = step[0]
                    split_ahead(step_start[l, at])
                    if kind == "lin":
                        part, t = step[1:]
                        name = f"{part}{l}.{t}"
                        if part == "lg":
                            evac(name, UC[:, t, lo:TT], ACT.Sigmoid)
                        elif part == "q":
                            evac(name, Q[:, t, lo:TT])
                        elif part == "k":
                            evac(name, K[:, t, :])
                        elif part == "p":
                            evac(name, PL[:, t, s0:2, 8:8 + S], src=segments(bank(name)[:, 0:TT - lo]))
                    elif kind == "v":
                        c, i = step[1:]
                        name = f"v{l}.{c}.{i}"
                        job_done(act, name)
                        swapped = value_tile[l, c] % NSPLIT > (value_tile[l, c] + 1) % NSPLIT
                        for half in range(2):
                            src = bank(name)[:, :].rearrange("p (i h n) -> p i h n", i=2, h=2)[:, :, half ^ swapped]
                            ins = act.activation(VV[:, i:i + 2, 256 * c + 128 * half:256 * c + 128 * half + 128], src,
                                                 ACT.Copy)
                        ins.then_inc(bank_signal(name)[0], 1)
                    elif kind == "mod" and step[3] == KT - 1:
                        mod_rows(*step[1:3])
                    elif kind == "rot" and step[1] == 0:
                        evac(f"lam{l}", LAME, ACT.Exp)
                    elif kind == "Z":
                        gi = step[1]
                        hd, blocks, nk = groups[gi]
                        if gi == 0:
                            act.wait_ge(pad_zeroed, l + 2)
                        if gi >= 2:
                            pd = groups[gi - 2]
                            job_done(act, f"s{l}.{gi - 2}.{pd[1][1]}.1")
                        act.wait_ge(rotated, 4 * l + hd // 2 + 1)
                        c0 = blocks[0] * 128
                        act.activation(SQ[0:64, gi % 2, 0:S], Q[0:64, hd, c0:c0 + S], ACT.Copy)
                        act.activation(SQ[64:128, gi % 2, S:TT], Q[64:128, hd, c0:c0 + S], ACT.Copy)\
                            .then_inc(q_padded, 1)
                    elif kind == "S":
                        gi = step[1]
                        hd, blocks, nk = groups[gi]
                        for j, b in enumerate(blocks):
                            for comp in range(2):
                                nxt(max_set)
                                st = ST[:, gi % 2, j, comp, :]
                                evac(f"s{l}.{gi}.{b}.{comp}", PR[:, gi % 2, j, comp, 0:nk], ACT.Exp,
                                     bias=st[:, 1:2], scale=0.125, accum_out=st[:, 2:3])
                    elif kind == "T":
                        gi = step[1]
                        hd, blocks, nk = groups[gi]
                        for j, b in enumerate(blocks):
                            name = f"pt{l}.{gi}.{b}"
                            evac(name, PR[:, gi % 2, j, 1, 0:nk])
                    elif kind == "O":
                        gi = step[1]
                        hd, blocks, nk = groups[gi]
                        evac(f"o{l}.{gi}", Q[:, hd, blocks[0] * 128:blocks[0] * 128 + S])
                    elif kind == "var":
                        for t in range(4):
                            nxt(centred)
                            square(UC[:, t, lo:TT])
                    elif kind == "conv_root":
                        root(f"var{l}", TT - lo, 512)
                        for t in range(4):
                            nxt(conv_scaled)
                            act.activation(UC[:, t, lo:TT], UC[:, t, lo:TT], ACT.Silu, bias=C(f"ln_b{l}", t),
                                           scale=C(f"ln_g{l}", t)).then_inc(conv_act, 1)
                    elif kind == "square":
                        for gi, g in enumerate(groups):
                            if g[0] == step[1]:
                                evacuated(act, f"o{l}.{gi}")
                        square(Q[:, step[1], lo:TT])
                    elif kind == "sub_root":
                        if step[1] >= 2:
                            act.wait_ge(heads_normed, KT * l + step[1] - 1)
                        root(f"sub{l}.{step[1]}", TT - lo, 128)
                    elif kind == "gate":
                        br, t = step[1:]
                        if len(ring_user) >= 4:
                            evacuated(act, ring_user[-4])
                        ring_user.append(f"y{l}.{br}.{t}")
                        evac(f"g{l}.{br}.{t}", GR[:, t % 4, lo:TT], ACT.Sigmoid, bias=C(f"b_gate{l}", 8 * br + t))
                    elif kind == "pool" and step[1] == 0:
                        job_done(act, "pm0.3" if l else "adaT2.2")
                        act.dma_start(POOLW, a["w_pool_group_2"][l].rearrange("g c d -> c g d")).then_inc(poolw_in, 16)
                    elif kind == "mix":
                        for t in range(4):
                            evac(f"pm{l}.{t}", PO[:, t, lo:TT], ACT.Copy, scale=C(f"pool_scale{l}", t))
                for t in range(KT):
                    evac(f"m{l}.{t}", Q[:, t, lo:TT])
                    evacuated(act, f"m{l}.{t}")
                    square(Q[:, t, lo:TT])
                    split_ahead(jobs[f"m{l}.{t}"] + 1)
                root(f"post{l}", TT - lo, D)
                for t in range(KT):
                    nxt(x_set)
                    square(X[:, t, lo:TT])
                root(f"ffn{l}", TT - lo, D)
                shift_hi(1 + l, lo, 24)
                for c in range(HALF):
                    for part in ("fg", "fu"):
                        for t in (2 * c, 2 * c + 1):
                            split_ahead(jobs[f"{part}{l}.{t}"])
                            if part == "fg":
                                evac(f"fg{l}.{t}", FA[:, t, lo:TT], ACT.Silu)
                for t in range(KT):
                    evac(f"f{l}.{t}", M[:, t, lo:TT])
                    evacuated(act, f"f{l}.{t}")
                    square(M[:, t, lo:TT])
                root(f"out{l}", TT - lo, D)

            act.wait_ge(consts_in, 32)
            act.activation(CSIG, C("c", 0, 24), ACT.Sigmoid).then_inc(silu_sig, 1)
            if "a" in phases:
                block1()
            if "b" in phases:
                moe()
            if "c" in phases:
                for l in range(LAYERS):
                    layer(l)

        @block.vector
        def _(dve):
            nxt = Next(dve)

            def link(ins, s=None):
                s = dve_chain if s is None else s
                ins.then_inc(s, 1)
                dve.wait_ge(s, count(s))

            def link_bank(ins, name):
                s, v = bank_signal(name)
                ins.then_inc(s, 1)
                dve.wait_ge(s, v)

            def stt(out, in0, scalar, in1, op0, op1, **kw):
                return dve.scalar_tensor_tensor(out=out, in0=in0, scalar=scalar, in1=in1, op0=op0, op1=op1, **kw)

            def mod_columns(n, q):
                name = f"adaT{n}.{q}"
                job_done(dve, name)
                src = bank(name)[:, :].rearrange("p (s j m) -> p j s m", s=4, j=4)
                bias = C(f"b_ada{n}", 16 * q, 16).rearrange("p (j s) -> p j s", s=4)
                ms = ((0, 0),) if n == 0 else ((0, 1), (1, 2))
                for m, col in ms:
                    out = ADA[:, n, m, 16 * q:16 * q + 16].rearrange("p (j s) -> p j s", s=4)
                    i = dve.tensor_tensor(out, src[:, :, :, col], bias, ADD)
                    if m == ms[-1][0]:
                        link_bank(i, name)
                    else:
                        link(i)

            def pre_scale(n, gain, first):
                for m in range(1 if n == 0 else 2):
                    link(stt(CF[:, m, :], ADA[:, n, m, first:first + KT], 1.0, C(gain, 0, KT), ADD, MUL))

            def post_scale(n, gain, first):
                for m in range(1 if n == 0 else 2):
                    link(dve.tensor_tensor(CF[:, m, :], ADA[:, n, m, first:first + KT], C(gain, 0, KT), MUL))

            def inverse_rms(name, width):
                nxt(rs_set)
                return RS[:, rms_buffer[name], 0:width]

            def split_norm(name, n, lo, first):
                rs = inverse_rms(name, TT - lo)
                for t in range(KT + 1):
                    if t < KT:
                        for a0, b0, m in parts_of(lo):
                            i = stt(M[:, t, a0:b0], X[:, t, a0:b0], CF[:, m, t:t + 1], rs[:, a0 - lo:b0 - lo],
                                    MUL, MUL)
                            link(i, scaled if b0 == TT else None)
                    if t:
                        nxt(h_hi_set)
                        for a0, b0, m in parts_of(lo):
                            i = stt(HL[:, t - 1, a0:b0], M[:, t - 1, a0:b0],
                                    ADA[:, n, m, first + t - 1:first + t], HH[:, t - 1, a0:b0], ADD, SUB)
                            link(i, h_lo_set if b0 == TT else None)

            def pre_norm(name, out, off, lo):
                rs = inverse_rms(name, TT - lo)
                for t in range(KT):
                    for a0, b0, m in parts_of(lo):
                        i = stt(out[:, t, a0 - off:b0 - off], X[:, t, a0:b0], CF[:, m, t:t + 1],
                                rs[:, a0 - lo:b0 - lo], MUL, MUL)
                        if b0 == TT:
                            link(i, scaled)
                        else:
                            link(i)

            def post_norm(name, src, off, lo):
                rs = inverse_rms(name, TT - lo)
                for t in range(KT):
                    for a0, b0, m in parts_of(lo):
                        link(stt(tmp[:, a0 - lo:b0 - lo], src[:, t, a0 - off:b0 - off], CF[:, m, t:t + 1],
                                 rs[:, a0 - lo:b0 - lo], MUL, MUL))
                    link(dve.tensor_tensor(X[:, t, lo:TT], X[:, t, lo:TT], tmp[:, 0:TT - lo], ADD), x_set)

            def softplus():
                x = C("lam", 0, 8)
                al, e, w, ln, d, z, r, v, y, o = (SP[:, i, :] for i in range(10))
                link(stt(al, x, -1.0, x, MUL, MAX), sp_abs)
                nxt(sp_exp)
                link(dve.tensor_scalar(w, e, 1.0, None, ADD), sp_one)
                link(dve.tensor_scalar(d, w, -1.0, None, ADD))
                link(dve.tensor_scalar(z, d, 0.0, None, ALU.is_equal))
                link(dve.tensor_tensor(d, d, z, ADD))
                link(dve.reciprocal(r, d))
                nxt(sp_ln)
                link(dve.tensor_tensor(v, ln, e, MUL))
                link(dve.tensor_tensor(v, v, r, MUL))
                link(dve.tensor_tensor(y, z, e, MUL))
                link(dve.tensor_tensor(v, v, y, ADD))
                link(dve.tensor_scalar(o, x, -1.0, 0.0, MUL, MAX))
                link(dve.tensor_tensor(v, v, o, ADD))
                link(dve.tensor_scalar(K8, v, -8.0, None, MUL))
                link(dve.tensor_scalar(P4, v, 4.0, None, MUL), sp_set)

            def block1():
                softplus()
                link(dve.tensor_scalar(QB, C("b_in", 16, 8), 0.125, None, MUL), q_bias_set)
                link(dve.memset(XR[:, :, 0:3], 0.0))
                mod_columns(0, 0)
                pre_scale(0, "pre_mix", 8)
                link(dve.tensor_copy(tmp[:, 0:1], ones[:, 0:1]), ada_set)
                pre_norm("b1.pre", H1, S, S)
                link(dve.memset(SQ[64:128, 0, 0:S], 0.0))
                link(dve.memset(SQ[0:64, 1, 0:S], 0.0), pad_zeroed)
                dve.wait_ge(dist_in, 16)
                for step in block1_steps():
                    kind = step[0]
                    if kind == "lin" and step[1] == "xr":
                        t = step[2]
                        evacuated(dve, f"xr{t}")
                        link(dve.tensor_scalar(XC[:, t, :], XR[:, t, 0:S], C("conv_w", t), C("conv_b", t), MUL, ADD))
                        for k in range(1, 4):
                            link(stt(XC[:, t, :], XR[:, t, k:k + S], C("conv_w", 8 * k + t), XC[:, t, :], MUL, ADD),
                                 conv1_set if (t, k) == (KT - 1, 3) else None)
                    elif kind == "lin" and step[1] == "yr":
                        t = step[2]
                        evacuated(dve, f"sr{t}")
                        job_done(dve, f"yr{t}")
                        link_bank(dve.tensor_tensor(M1[:, t, :], bank(f"yr{t}")[:, 0:S], SR[:, t, :], MUL), f"yr{t}")
                    elif kind == "lin" and step[1] == "ya":
                        t = step[2]
                        job_done(dve, f"ya{t}")
                        link_bank(dve.tensor_tensor(tmp[:, 0:S], bank(f"ya{t}")[:, 0:S], SA[:, t, :], MUL), f"ya{t}")
                        link(dve.tensor_tensor(M1[:, t, :], M1[:, t, :], tmp[:, 0:S], ADD), merged)
                    elif kind == "modT":
                        mod_columns(*step[1:])
                    elif kind == "mult":
                        evacuated(dve, "gi7")
                        n = KT * S
                        mu, gi = flat(MU), flat(GI)
                        link(dve.tensor_tensor(gi, gi, flat(XC), MUL))
                        dve.wait_ge(mult_set, 1)
                        link(stt(mu, flat(GA), 1.0, mu, ADD, MUL))
                        link(dve.memset(MU[:, :, 0:1], 1.0))
                        link(dve.tensor_tensor(gi, gi, mu, MUL))
                        for t in range(KT):
                            link(dve.tensor_tensor_scan(XC[:, t, :], GA[:, t, :], GI[:, t, :], 0.0, MUL, ADD))
                        link(dve.tensor_tensor(flat(GG), flat(GG), flat(XC), MUL), rnn_set)
                    elif kind == "S":
                        hd = step[1]
                        job_done(dve, f"s{hd}")
                        if hd >= 2:
                            job_done(dve, f"pt{hd - 2}")
                        st = ST1[:, hd % 2]
                        link_bank(stt(P1[:, hd % 2, :], DIST, -slopes[hd], bank(f"s{hd}")[:, 0:NDIST], MUL, ADD),
                                  f"s{hd}")
                        link(dve.reduce_max(st[:, 0, 0:1], P1[:, hd % 2, 0:128], axis=AX.X))
                        link(dve.reduce_max(st[:, 0, 1:2], P1[:, hd % 2, 128:384], axis=AX.X))
                        link(dve.tensor_scalar(st[:, 1, :], st[:, 0, :], C("sinks", hd), -1.0, MAX, MUL), max_set)
                    elif kind == "T":
                        hd = step[1]
                        st = ST1[:, hd % 2]
                        nxt(prob_set)
                        link(dve.tensor_tensor(st[:, 2, :], st[:, 2, :], st[:, 3, :], ADD))
                        link(dve.reciprocal(st[:, 2, :], st[:, 2, :]))
                        link(dve.tensor_scalar(P1[:, hd % 2, 0:128], P1[:, hd % 2, 0:128], st[:, 2, 0:1], None, MUL))
                        link(dve.tensor_scalar(P1[:, hd % 2, 128:384], P1[:, hd % 2, 128:384], st[:, 2, 1:2], None,
                                               MUL), prob_normed)
                post_scale(0, "post_mix", 16)
                post_norm("b1.post", MX1, S, S)
                pre_scale(0, "pre_ffn", 32)
                pre_norm("b1.ffn", H2, S, S)

            def select(e, slots, bpar):
                for i in range(2):
                    pos, gate = POS[:, i, bass.ds(e, 1)], GATE[:, i, bass.ds(e, 1)]
                    dve.tensor_scalar(PSEL[:, i, :], slots(0, SLOT), pos, None, ALU.is_equal)
                    for half in range(2):
                        dve.tensor_scalar(GSEL[:, i, half, :], slots(128 * half, 128), pos, gate, ALU.is_equal, MUL)
                dve.tensor_scalar(BSEL[:, bpar, :], ones[:, 0:SLOT], ident[:, bass.ds(e, 1)], None, MUL)\
                    .then_inc(sel_set, 1)

            def swiglu(n, read):
                dve.wait_ge(moe_read, read)
                h = [ps[b][:, :].rearrange("p (f two) -> p f two", two=2) for b in range(2)]
                for b in range(2):
                    i = dve.tensor_scalar(GLU[:, 256 * b:256 * b + 256], h[b][:, :, 0], LIMIT, None, MIN)
                i.then_inc(glu_set, 1)
                for b in range(2):
                    i = dve.tensor_scalar(LIN[:, 256 * b:256 * b + 256], h[b][:, :, 1], LIMIT, -LIMIT, MIN, MAX)
                i.then_inc(lin_set, 1)
                dve.wait_ge(lin_set, n + 1)
                dve.wait_ge(sig_set, n + 1)
                dve.tensor_tensor(AC, GLU, SIG, MUL).then_inc(half_act, 1)
                dve.wait_ge(half_act, n + 1)
                stt(AC, LIN, 1.0, AC, ADD, MUL).then_inc(act_set, 1)

            def add_rows(n, sc):
                for r in range(2):
                    dve.wait_ge(scattered, sc + r)
                    for half in range(2):
                        f0 = 4 * half + 2 * r
                        v = V(4096 + f0 * S, 2 * S)
                        i = dve.tensor_tensor(v, v, ps[(0, 6)[r] + half][:, :], ADD)
                    i.then_inc((added0, added1)[r], 1)
                dve.wait_ge(added1, n + 1)

            def moe():
                dve.wait_ge(moe_consts_in, 16 * 4)
                link(dve.memset(LG[:, :, NE:NE + 8], -BIG))
                link(dve.memset(M8[:, :, 12:16], -BIG))
                link(dve.memset(GATE[:, :, NE:NE + 2], 0.0))
                link(dve.memset(POS[:, :, NE:NE + 2], -1.0))
                for i in range(2):
                    job_done(dve, f"lg{i}")
                    link_bank(dve.tensor_copy(LG[:, i, 0:NE], bank(f"lg{i}")[:, 0:NE]), f"lg{i}")
                    link(dve.max(M8[:, i, 0:8], LG[:, i, 0:NE]))
                    link(dve.tensor_scalar(GST[:, i, 0:1], M8[:, i, 0:1], -1.0, None, MUL), rmax_set)
                    link(dve.tensor_copy(M8[:, i, 8:12], M8[:, i, 0:4]))
                    link(dve.match_replace(LR[:, i, :], M8[:, i, 8:16], LG[:, i, :], BIG))
                    link(dve.tensor_tensor(MK[:, i, :], LR[:, i, 0:NE], LG[:, i, 0:NE], ALU.not_equal), mask_set)
                for i in range(2):
                    nxt(rexp_set)
                    link(dve.tensor_tensor(EX[:, i, :], EX[:, i, :], MK[:, i, :], MUL))
                    link(dve.reduce_sum(GST[:, i, 1:2], EX[:, i, :], axis=AX.X))
                    link(dve.reciprocal(GST[:, i, 2:3], GST[:, i, 1:2]))
                    link(dve.tensor_scalar(GATE[:, i, 0:NE], EX[:, i, :], GST[:, i, 2:3], None, MUL), gate_set)
                for i in range(2):
                    job_done(dve, f"pos{i}")
                    link_bank(stt(POS[:, i, 0:NE], bank(f"pos{i}")[:, 0:NE], 1.0, MK[:, i, :], ADD, MUL), f"pos{i}")
                    link(dve.tensor_scalar(POS[:, i, 0:NE], POS[:, i, 0:NE], -1.0, None, ADD))
                job_done(dve, "cnt")
                for r in range(3):
                    i = dve.tensor_scalar(OFLAG[0:1, r * NE:(r + 1) * NE], bank("cnt")[0:1, 0:NE],
                                          float(SLOT * (r + 1)), None, ALU.is_gt)
                    if r < 2:
                        link(i)
                    else:
                        link_bank(i, "cnt")
                for j in range(4):
                    job_done(dve, f"b2{j}")
                    link_bank(dve.tensor_copy(V(4096 + 2 * j * S, 2 * S), bank(f"b2{j}")[:, :]),
                              f"b2{j}")

                def first(c0, n):
                    return route_table("slots")[:, c0:c0 + n]

                select(0, first, 0)
                dve.wait_ge(gathered, 1)
                dve.wait_ge(gate_turned, 1)
                select(1, first, 1)
                link(dve.tensor_tensor_scan(OCUM[0:1, :], ones[0:1, 0:OVER], OFLAG[0:1, :], 0.0, MUL, ADD))
                link(dve.tensor_tensor(OEXP[0:1, :], OFLAG[0:1, :], route_table("expert_of")[0:1, :], MUL))
                link(dve.tensor_tensor(ORND[0:1, :], OFLAG[0:1, :], route_table("round_of")[0:1, :], MUL))
                for s in range(OVERMAX):
                    for at, src in ((0, OEXP), (OVERMAX, ORND)):
                        link(stt(OJUNK[0:1, :], OCUM[0:1, :], float(s + 1), src[0:1, :], ALU.is_equal, MUL,
                                 accum_out=OLIST[0:1, at + s:at + s + 1]))
                link(dve.tensor_copy(lists[0:1, 0:2 * OVERMAX], OLIST[0:1, :]))
                link(dve.tensor_copy(lists[0:1, 2 * OVERMAX:2 * OVERMAX + 1], OCUM[0:1, OVER - 1:OVER]), lists_set)
                with dve.Fori(0, NE // 2) as it:
                    for u in range(2):
                        n = it * 2 + u
                        swiglu(n, it * (2 * EC) + EC * u + KT)
                        dve.wait_ge(gathered, n + 2)
                        dve.wait_ge(gate_turned, n + 2)
                        select(n + 2, first, u)
                        add_rows(n, it * 4 + 2 * u + 1)
                n_over = dve.value_load(lists[0:1, 2 * OVERMAX:2 * OVERMAX + 1], min_val=0, max_val=OVERMAX)
                dve.wait_ge(sel_set, NE + 2)
                with dve.If(n_over > 0):
                    with dve.Fori(0, n_over) as q:
                        e = dve.value_load(lists[0:1, bass.ds(q, 1)], min_val=0, max_val=NE - 1)
                        r = dve.value_load(lists[0:1, bass.ds(q + OVERMAX, 1)], min_val=0, max_val=3)
                        select(e, lambda c0, n: work[:, bass.ds(r * 256 + (rt_at - FRONT + c0), n)], 0)
                        swiglu(q + NE, q * EC + (EC * NE + KT))
                        add_rows(q + NE, q * 2 + (2 * NE + 1))
                with dve.Else():
                    pass
                link(dve.tensor_copy(tmp[:, 0:1], ones[:, 0:1]), ff_done)
                post_scale(0, "post_ffn", 40)
                post_norm("b1.out", FF, S, S)

            def conv_taps(l, t, part):
                s0 = 0 if l == 0 else 1
                if part == 0:
                    evacuated(dve, f"la{l}.{t}")
                out = segments(UC[:, t, s0 * S:TT])
                for k in range(8 * part, min(8 * part + 8, TAPS)):
                    src = U[:, t, s0:2, k:k + S]
                    if k == 0:
                        link(dve.tensor_scalar(out, src, C(f"taps{l}", t), C(f"tap_b{l}", t), MUL, ADD))
                    else:
                        link(stt(out, src, C(f"taps{l}", 4 * k + t), out, MUL, ADD),
                             convolved if k == TAPS - 1 else None)

            def pooling(l, g):
                lo = 0 if l == 0 else S
                s0 = lo // S
                if g == 0:
                    job_done(dve, f"o{l}.{len(groups_of(l)) - 1}")
                evacuated(dve, f"p{l}.{g}")
                src = PL[:, g, s0:2, :]
                n = S + 16
                for i in range(g + 1):
                    dst = (PA, PB)[i % 2][:, s0:2, :]
                    n -= 1 << i
                    link(dve.tensor_tensor(dst[:, :, 0:n], src[:, :, 0:n], src[:, :, 1 << i:n + (1 << i)], ADD))
                    src = dst
                w = 2 << g
                out = segments(PO[:, g, lo:TT])
                link(dve.tensor_scalar(out, src[:, :, 8 - w // 2:8 - w // 2 + S], 1.0 / w, None, MUL))
                for e0, c0 in ((0, 0), (8, S - 8)):
                    for s in range(2 - s0):
                        v = out[:, s, c0:c0 + 8]
                        link(dve.tensor_tensor(v, v, edge[:, g, e0:e0 + 8], MUL))
                link(dve.tensor_tensor(out, out, PL[:, g, s0:2, 8:8 + S], SUB), pooled)

            def layer(l):
                lo = 0 if l == 0 else S
                s0 = lo // S
                n = 1 + l
                width = TT - lo
                pre_scale(n, f"pre_mix{l}", 8)
                split_norm(f"pre{l}", n, 0, 0)
                link(dve.memset(SQ[64:128, :, 0:S], 0.0))
                link(dve.memset(SQ[0:64, :, S:TT], 0.0), pad_zeroed)
                qk = C(f"lam_qk{l}", 0, 4).rearrange("p (n two) -> p n two", two=2)
                link(dve.tensor_tensor(LAMP, qk[:, :, 0], qk[:, :, 1], MUL), lam_prod)
                link(dve.tensor_scalar(SUBG, C(f"subln{l}"), 1.0 - lam_init[l], None, MUL))
                link(dve.memset(U[:, :, :, 0:TAPS // 2], 0.0))
                link(dve.memset(U[:, :, :, S + TAPS // 2:S + TAPS - 1], 0.0))
                link(dve.memset(PL[:, :, :, 0:8], 0.0))
                link(dve.memset(PL[:, :, :, S + 8:S + 16], 0.0))
                groups = groups_of(l)
                for step in layer_steps(l):
                    kind = step[0]
                    if kind == "lin" and step[1] == "la":
                        t = step[2]
                        evacuated(dve, f"lg{l}.{t}")
                        name = f"la{l}.{t}"
                        job_done(dve, name)
                        link_bank(dve.tensor_tensor(U[:, t, s0:2, TAPS // 2:TAPS // 2 + S],
                                                    segments(bank(name)[:, 0:width]), segments(UC[:, t, lo:TT]), MUL),
                                  name)
                    elif kind == "conv":
                        conv_taps(l, *step[1:])
                    elif kind == "pool":
                        pooling(l, step[1])
                    elif kind == "rot":
                        for t in (2 * step[1], 2 * step[1] + 1):
                            for part, view in (("q", Q), ("k", K)):
                                name = f"rot{part}{l}.{t}"
                                job_done(dve, name)
                                link_bank(dve.tensor_tensor(tmp[:, 0:S], bank(name)[:, 0:S], sin, MUL), name)
                                link(dve.tensor_tensor(view[:, t, S:TT], view[:, t, S:TT], cos, MUL))
                                link(dve.tensor_tensor(view[:, t, S:TT], view[:, t, S:TT], tmp[:, 0:S], ADD),
                                     rotated if (t % 2, part) == (1, "k") else None)
                        if step[1] == 0:
                            evacuated(dve, f"lam{l}")
                            link(dve.tensor_scalar(NLAM, LAME[:, 1:2], lam_init[l], LAME[:, 0:1], SUB, SUB))
                    elif kind == "modT":
                        mod_columns(*step[1:])
                    elif kind == "S":
                        gi = step[1]
                        hd, blocks, nk = groups[gi]
                        for j, b in enumerate(blocks):
                            for comp in range(2):
                                name = f"s{l}.{gi}.{b}.{comp}"
                                job_done(dve, name)
                                st = ST[:, gi % 2, j, comp, :]
                                link(dve.reduce_max(st[:, 0:1], bank(name)[:, 0:nk], axis=AX.X))
                                link(dve.tensor_scalar(st[:, 1:2], st[:, 0:1], -0.125, None, MUL), max_set)
                    elif kind == "T":
                        gi = step[1]
                        hd, blocks, nk = groups[gi]
                        for j, b in enumerate(blocks):
                            p = [PR[:, gi % 2, j, comp, 0:nk] for comp in range(2)]
                            st = [ST[:, gi % 2, j, comp, :] for comp in range(2)]
                            evacuated(dve, f"s{l}.{gi}.{b}.0")
                            evacuated(dve, f"s{l}.{gi}.{b}.1")
                            link(dve.reciprocal(ST[:, gi % 2, j, :, 3:4], ST[:, gi % 2, j, :, 2:3]))
                            link(dve.tensor_tensor(st[1][:, 4:5], st[1][:, 3:4], NLAM, MUL))
                            link(dve.tensor_scalar(p[0], p[0], st[0][:, 3:4], None, MUL))
                            link(stt(p[0], p[1], st[1][:, 4:5], p[0], MUL, ADD), prob_normed)
                    elif kind == "mean":
                        name = f"mean{l}"
                        job_done(dve, name)
                        link_bank(dve.tensor_scalar(tmp[:, 0:width], bank(name)[:, 0:width], 1.0 / 512, None, MUL),
                                  name)
                        for t in range(4):
                            link(dve.tensor_tensor(UC[:, t, lo:TT], UC[:, t, lo:TT], tmp[:, 0:width], SUB), centred)
                    elif kind == "conv_root":
                        rs = inverse_rms(f"var{l}", width)
                        for t in range(4):
                            link(dve.tensor_tensor(UC[:, t, lo:TT], UC[:, t, lo:TT], rs[:, 0:width], MUL), conv_scaled)
                    elif kind == "sub_root":
                        hd = step[1]
                        rs = inverse_rms(f"sub{l}.{hd}", width)
                        link(stt(Q[:, hd, lo:TT], Q[:, hd, lo:TT], SUBG, rs[:, 0:width], MUL, MUL), heads_normed)
                    elif kind == "y":
                        br, t = step[1:]
                        name = f"y{l}.{br}.{t}"
                        evacuated(dve, f"g{l}.{br}.{t}")
                        job_done(dve, name)
                        out = M[:, t, lo:TT] if br == 0 else tmp[:, 0:width]
                        link_bank(dve.tensor_tensor(out, bank(name)[:, 0:width], GR[:, t % 4, lo:TT], MUL), name)
                        if br:
                            link(dve.tensor_tensor(M[:, t, lo:TT], M[:, t, lo:TT], out, ADD),
                                 merged if br == 2 else None)
                post_scale(n, f"post_mix{l}", 16)
                post_norm(f"post{l}", Q, 0, lo)
                pre_scale(n, f"pre_ffn{l}", 32)
                split_norm(f"ffn{l}", n, lo, 24)
                for t in range(FT):
                    name = f"fu{l}.{t}"
                    evacuated(dve, f"fg{l}.{t}")
                    job_done(dve, name)
                    link_bank(dve.tensor_tensor(FA[:, t, lo:TT], FA[:, t, lo:TT], bank(name)[:, 0:width], MUL), name)
                post_scale(n, f"post_ffn{l}", 40)
                post_norm(f"out{l}", M, 0, lo)

            link(dve.memset(EPSC, EPS), eps_set)
            link(dve.memset(cstat[:, :], 0.0))
            dve.wait_ge(silu_sig, 1)
            link(dve.tensor_tensor(CS[:, :, 0:3].rearrange("p k m -> p m k"), C("c", 0, 24).rearrange("p (m k) -> p m k", m=3),
                                   CSIG.rearrange("p (m k) -> p m k", m=3), MUL), silu_set)
            if "a" in phases:
                block1()
            if "b" in phases:
                moe()
            if "c" in phases:
                for l in range(LAYERS):
                    layer(l)


def column_array(inputs):
    out = np.zeros((128, NCOL), np.float32)

    def put(name, v, at=0):
        v = np.asarray(v).reshape(-1, 128).T
        c = COLS[name][0] + at
        out[:, c:c + v.shape[1]] = v

    put("c", inputs["c"])
    put("c", inputs["c_2"], 8)
    put("c", inputs["c_ctx_2"], 16)
    put("b_ada0", inputs["b_ada"])
    put("b_ada1", inputs["b_mod_2"][0])
    put("b_ada2", inputs["b_mod_2"][1])
    for name, src in (("pre_mix", "norm_pre_mix"), ("post_mix", "norm_post_mix"), ("pre_ffn", "norm_pre_ffn"),
                      ("post_ffn", "norm_post_ffn"), ("b_in", "b_in"), ("conv_w", "conv_w"), ("conv_b", "conv_b"),
                      ("b_a", "rg_b_a"), ("b_x", "rg_b_x"), ("lam", "rg_lambda")):
        put(name, inputs[src])
    bk = np.asarray(inputs["b_in"])[0, 3072:3328].reshape(4, 64)
    put("bk", np.concatenate([bk, bk], axis=1))
    c = COLS["sinks"][0]
    out[:, c:c + 16] = np.asarray(inputs["attn_sinks"])
    for l in range(LAYERS):
        for name, src in (("pre_mix", "g_pre_mix_2"), ("post_mix", "g_post_mix_2"), ("pre_ffn", "g_pre_ffn_2"),
                          ("post_ffn", "g_post_ffn_2"), ("b_gate", "b_gate_2"), ("taps", "conv_w_2"),
                          ("tap_b", "conv_b_2"), ("ln_g", "conv_ln_g_2"), ("ln_b", "conv_ln_b_2"),
                          ("subln", "subln_g_2"), ("pool_scale", "pool_scale_2")):
            put(f"{name}{l}", inputs[src][l])
        c = COLS[f"lam_qk{l}"][0]
        for i, src in enumerate(("lam_q1_2", "lam_k1_2", "lam_q2_2", "lam_k2_2")):
            out[0:64, c + i] = np.asarray(inputs[src][l])
    return out


def kept_tables():
    out = np.zeros((128, NKEPT), np.float32)
    out[:, 0:128] = np.eye(128)
    f = np.arange(128)
    low = f % 32 < 16
    out[f[low] + 16, 128 + f[low]] = -1.0
    out[f[~low] - 16, 128 + f[~low]] = 1.0
    t = np.arange(S)
    inv = (10000.0 ** (-np.arange(0, 32, 2, dtype=np.float32) / 32)).astype(np.float32)
    place = np.where((f % 64 < 32)[:, None], (t // 64)[None], (t % 64)[None]).astype(np.float32)
    angle = place * inv[f % 16][:, None]
    out[:, 256:512] = np.cos(angle)
    out[:, 512:768] = np.sin(angle)
    for g in range(4):
        w = 2 << g
        t = np.concatenate([np.arange(8), np.arange(S - 8, S)])
        n = np.minimum(t + w // 2, S) - np.maximum(t - w // 2, 0)
        out[:, 768 + 16 * g:784 + 16 * g] = w / n
    return out


def route_tables():
    out = np.zeros((128, NROUTE), np.float32)
    none = np.full(SLOT, -2.0)
    for r in range(4):
        s = SLOT * r + np.arange(SLOT)
        out[:, 256 * r:256 * (r + 1)] = np.concatenate([s, none, none, s])
    out[:, 1024:1152] = np.triu(np.ones((128, 128)), 1)
    out[:, 1152:1152 + OVER] = np.arange(OVER) % NE
    out[:, 1152 + OVER:] = np.arange(OVER) // NE + 1
    return out


def distances():
    q, c = np.arange(128)[:, None], np.arange(128)[None]
    near = q - c
    dist = np.concatenate([near, near + 128, near], axis=1).astype(np.float32)
    return np.where((dist >= 0) & (dist < 128), dist, np.float32(FAR)).astype(np.float32)


def laid_out(inputs):
    arrays = {"cols": column_array(inputs), "kept": kept_tables(), "route": route_tables(), "dist": distances()}
    arrays["rows"] = np.concatenate([np.asarray(inputs["b_in"])[0, 3328:3584],
                                     np.asarray(inputs["router_b"])[0]])[None]
    arrays["x"] = np.ascontiguousarray(np.asarray(inputs["x"])[0].T)
    arrays["ctx"] = np.ascontiguousarray(np.asarray(inputs["ctx_2"])[0].T)
    for name in ("w_ada", "w_in", "rg_w_a", "rg_w_x", "w_o_rnn", "w_o_attn", "w_out", "router_w",
                 "moe_w1", "moe_w2", "moe_b1", "moe_b2"):
        arrays[name] = np.asarray(inputs[name])[0]
    for name in ("w_mod_2", "w_in_2", "w_conv_out_2", "w_attn_out_2", "w_pool_group_2", "w_pool_out_2",
                 "w_out_2", "w_ffn_in_2", "w_ffn_out_2"):
        arrays[name] = np.asarray(inputs[name])
    return arrays


def kernel(**inputs):
    import concourse.bacc as bacc
    from concourse.bass_utils import run_bass_kernel_spmd

    nc = bacc.Bacc("TRN2", target_bir_lowering=False, num_devices=1)
    arrays = laid_out(inputs)
    aps = {name: nc.dram_tensor(f"in_{name}", v.shape, mybir.dt.from_np(v.dtype), kind="ExternalInput").ap()
           for name, v in arrays.items()}
    aps["out"] = nc.dram_tensor("out_t", (D, S), mybir.dt.float32, kind="ExternalOutput").ap()
    build_program(nc, aps)
    r = run_bass_kernel_spmd(nc, [{f"in_{name}": v for name, v in arrays.items()}], core_ids=[0])
    return np.ascontiguousarray(r.results[0]["out_t"].T)[None]
```
